# Optimizing a Trainium2 kernel written in Bass

```python
import jax, jax.numpy as jnp
from jax import lax
import numpy as np

D_MODEL = 2048
BATCH = 1
SEQ = 256
DEPTH = 1

HG_HEADS = 16
HG_KDIM = 128
HG_VDIM = D_MODEL // HG_HEADS
HG_FDIM = HG_HEADS * HG_KDIM
HG_VWIDTH = HG_HEADS * HG_VDIM
HG_CHUNK = 64
MLA_HEADS = 16
Q_LORA = 512
KV_LORA = 512
QK_NOPE = 128
QK_ROPE = 64
V_DIM = 128
QK_DIM = QK_NOPE + QK_ROPE
ROPE_THETA = 10000.0
ATTN_BLOCK = 128
FF_MULT = 256
D_FF = ((8 * D_MODEL + 3 * FF_MULT - 1) // (3 * FF_MULT)) * FF_MULT
N_MOD = 6
EPS = 1e-6
IN_SIZES = (HG_FDIM, HG_FDIM, HG_VWIDTH, HG_VWIDTH,
            Q_LORA, KV_LORA, QK_ROPE,
            D_MODEL, D_MODEL)
IN_WIDTH = sum(IN_SIZES)

kernel_name = "hybrid_hgrn2_mla_swiglu_sandwich_adaln"

def rmsnorm(x, w):
    xf = x.astype(jnp.float32)
    y = xf * lax.rsqrt(jnp.mean(xf * xf, axis=-1, keepdims=True) + EPS)
    return (y * w.astype(jnp.float32)).astype(x.dtype)

def rope_tables(positions):
    inv_freq = ROPE_THETA ** (-jnp.arange(0, QK_ROPE, 2, dtype=jnp.float32) / QK_ROPE)
    ang = positions.astype(jnp.float32)[..., None] * inv_freq
    return jnp.cos(ang), jnp.sin(ang)

def apply_rope(t, cos, sin):
    cos = cos.astype(t.dtype)
    sin = sin.astype(t.dtype)
    t1, t2 = jnp.split(t, 2, axis=-1)
    return jnp.concatenate([t1 * cos - t2 * sin, t2 * cos + t1 * sin], axis=-1)

def hgrn2_chunked(q, k, v, g):
    B, S, H, K = q.shape
    V = v.shape[-1]
    C = HG_CHUNK
    nc = S // C

    def to_chunks(t):
        return t.reshape(B, nc, C, H, t.shape[-1]).transpose(1, 0, 3, 2, 4)

    tri = jnp.tril(jnp.ones((C, C), dtype=bool))[:, :, None]

    def step(state, inp):
        qc, kc, vc, gc = inp
        b = jnp.cumsum(gc, axis=2)
        o_inter = jnp.einsum('bhck,bhkv->bhcv', qc * jnp.exp(b), state)
        diff = b[:, :, :, None, :] - b[:, :, None, :, :]
        decay = jnp.exp(jnp.where(tri, diff, -jnp.inf))
        scores = jnp.einsum('bhtsk,bhsk->bhts', qc[:, :, :, None, :] * decay, kc)
        o_intra = jnp.einsum('bhts,bhsv->bhtv', scores, vc)
        b_last = b[:, :, -1:, :]
        state = (jnp.exp(b_last[:, :, 0, :])[..., None] * state
                 + jnp.einsum('bhck,bhcv->bhkv', kc * jnp.exp(b_last - b), vc))
        return state, o_inter + o_intra

    s0 = jnp.zeros((B, H, K, V), jnp.float32)
    _, o = lax.scan(step, s0, (to_chunks(q), to_chunks(k), to_chunks(v), to_chunks(g)))
    return o.transpose(1, 0, 3, 2, 4).reshape(B, S, H, V)

def causal_block_attention(q, k, v):
    B, S, H, Dq = q.shape
    nb = S // ATTN_BLOCK
    qb = q.reshape(B, nb, ATTN_BLOCK, H, Dq).transpose(1, 0, 2, 3, 4)
    k_pos = jnp.arange(S)
    scale = QK_DIM ** -0.5

    def one_block(args):
        q_blk, blk = args
        s = jnp.einsum('bqhd,bkhd->bhqk', q_blk, k,
                       preferred_element_type=jnp.float32) * scale
        q_pos = blk * ATTN_BLOCK + jnp.arange(ATTN_BLOCK)
        s = jnp.where(k_pos[None, :] <= q_pos[:, None], s, -jnp.inf)
        p = jax.nn.softmax(s, axis=-1).astype(v.dtype)
        return jnp.einsum('bhqk,bkhd->bqhd', p, v)

    out = lax.map(one_block, (qb, jnp.arange(nb)))
    return out.transpose(1, 0, 2, 3, 4).reshape(B, S, H, v.shape[-1])

def token_mixer(h, cos, sin, lb, w_in, g_hg_out, w_o_hg, g_q_lora, w_uq,
                g_kv_lora, w_ukv, w_o_mla, w_out):
    B, S, _ = h.shape
    dt = h.dtype
    f32 = jnp.float32
    split_idx = tuple(int(i) for i in np.cumsum(IN_SIZES)[:-1])
    hq, hf, hi, hg, cq, ckv, kr, gate_a, gate_b = jnp.split(h @ w_in, split_idx, axis=-1)

    q = jax.nn.silu(hq.astype(f32)).reshape(B, S, HG_HEADS, HG_KDIM)
    f = lb + (1.0 - lb) * jax.nn.sigmoid(hf.astype(f32))
    log_f = jnp.log(f).reshape(B, S, HG_HEADS, HG_KDIM)
    k = (1.0 - f).reshape(B, S, HG_HEADS, HG_KDIM)
    v = hi.astype(f32).reshape(B, S, HG_HEADS, HG_VDIM)
    o = hgrn2_chunked(q, k, v, log_f)
    o = rmsnorm(o, g_hg_out) * jax.nn.silu(hg.astype(f32)).reshape(B, S, HG_HEADS, HG_VDIM)
    y_a = o.reshape(B, S, HG_VWIDTH).astype(dt) @ w_o_hg

    q_m = (rmsnorm(cq, g_q_lora) @ w_uq).reshape(B, S, MLA_HEADS, QK_DIM)
    q_nope, q_rope = jnp.split(q_m, [QK_NOPE], axis=-1)
    kv = (rmsnorm(ckv, g_kv_lora) @ w_ukv).reshape(B, S, MLA_HEADS, QK_NOPE + V_DIM)
    k_nope, v_m = jnp.split(kv, [QK_NOPE], axis=-1)
    q_rope = apply_rope(q_rope, cos[:, :, None, :], sin[:, :, None, :])
    k_rope = apply_rope(kr, cos, sin)
    q_full = jnp.concatenate([q_nope, q_rope], axis=-1)
    k_full = jnp.concatenate(
        [k_nope, jnp.broadcast_to(k_rope[:, :, None, :], (B, S, MLA_HEADS, QK_ROPE))], axis=-1)
    att = causal_block_attention(q_full, k_full, v_m)
    y_b = att.reshape(B, S, MLA_HEADS * V_DIM) @ w_o_mla

    merged = jax.nn.sigmoid(gate_a) * y_a + jax.nn.sigmoid(gate_b) * y_b
    return merged @ w_out

def swiglu(h, w_gate_up, w_down):
    gate, up = jnp.split(h @ w_gate_up, 2, axis=-1)
    return (jax.nn.silu(gate) * up) @ w_down

def setup_inputs(seed: int = 0) -> dict:
    key = jax.random.key(seed)
    ks = jax.random.split(key, 24)
    f32 = jnp.float32

    def nrm(k, shape, scale):
        return jax.random.normal(k, shape, f32) * scale

    def gain(k, shape):
        return 1.0 + 0.02 * jax.random.normal(k, shape, f32)

    L = DEPTH
    x = jax.random.normal(ks[0], (BATCH, SEQ, D_MODEL), f32)
    c = jax.random.normal(ks[1], (BATCH, D_MODEL), f32)
    offset = jax.random.randint(ks[2], (BATCH, 1), 0, 4096, dtype=jnp.int32)
    positions = (jnp.arange(SEQ, dtype=jnp.int32)[None, :] + offset).astype(jnp.int32)
    return {
        "x": x,
        "c": c,
        "positions": positions,
        "w_ada": nrm(ks[3], (L, D_MODEL, N_MOD * D_MODEL), 0.5 * D_MODEL ** -0.5),
        "b_ada": nrm(ks[4], (L, N_MOD * D_MODEL), 0.01),
        "g_pre_mix": gain(ks[5], (L, D_MODEL)),
        "w_in": nrm(ks[6], (L, D_MODEL, IN_WIDTH), D_MODEL ** -0.5),
        "lb_logits": nrm(ks[7], (DEPTH + 1, HG_FDIM), 0.1),
        "g_hg_out": gain(ks[8], (L, HG_VDIM)),
        "w_o_hg": nrm(ks[9], (L, HG_VWIDTH, D_MODEL), HG_VWIDTH ** -0.5),
        "g_q_lora": gain(ks[10], (L, Q_LORA)),
        "w_uq": nrm(ks[11], (L, Q_LORA, MLA_HEADS * QK_DIM), Q_LORA ** -0.5),
        "g_kv_lora": gain(ks[12], (L, KV_LORA)),
        "w_ukv": nrm(ks[13], (L, KV_LORA, MLA_HEADS * (QK_NOPE + V_DIM)), KV_LORA ** -0.5),
        "w_o_mla": nrm(ks[14], (L, MLA_HEADS * V_DIM, D_MODEL), (MLA_HEADS * V_DIM) ** -0.5),
        "w_out": nrm(ks[15], (L, D_MODEL, D_MODEL), D_MODEL ** -0.5),
        "g_post_mix": gain(ks[16], (L, D_MODEL)),
        "g_pre_ffn": gain(ks[17], (L, D_MODEL)),
        "w_gate_up": nrm(ks[18], (L, D_MODEL, 2 * D_FF), D_MODEL ** -0.5),
        "w_down": nrm(ks[19], (L, D_FF, D_MODEL), D_FF ** -0.5),
        "g_post_ffn": gain(ks[20], (L, D_MODEL)),
    }

def reference(x, c, positions, w_ada, b_ada, g_pre_mix, w_in, lb_logits, g_hg_out,
              w_o_hg, g_q_lora, w_uq, g_kv_lora, w_ukv, w_o_mla, w_out, g_post_mix,
              g_pre_ffn, w_gate_up, w_down, g_post_ffn):
    lb_all = jnp.cumsum(jax.nn.softmax(lb_logits.astype(jnp.float32), axis=0), axis=0)
    cos, sin = rope_tables(positions)
    for l in range(DEPTH):
        mod = jax.nn.silu(c) @ w_ada[l] + b_ada[l]
        sh_m, sc_m, ga_m, sh_f, sc_f, ga_f = jnp.split(mod[:, None, :], N_MOD, axis=-1)
        h = rmsnorm(x, g_pre_mix[l]) * (1.0 + sc_m) + sh_m
        y = token_mixer(h, cos, sin, lb_all[l], w_in[l], g_hg_out[l], w_o_hg[l],
                        g_q_lora[l], w_uq[l], g_kv_lora[l], w_ukv[l], w_o_mla[l], w_out[l])
        x = x + ga_m * rmsnorm(y, g_post_mix[l])
        h = rmsnorm(x, g_pre_ffn[l]) * (1.0 + sc_f) + sh_f
        y = swiglu(h, w_gate_up[l], w_down[l])
        x = x + ga_f * rmsnorm(y, g_post_ffn[l])
    return x


_drawn_inputs = setup_inputs


def setup_inputs(seed=0):
    import zlib

    import numpy as np

    out = dict(_drawn_inputs(seed))
    spreads = {}
    factors = {'b_ada': 3.388,
     'g_pre_mix': 7.182,
     'lb_logits': 8.0,
     'g_hg_out': 8.0,
     'g_q_lora': 8.0,
     'g_kv_lora': 8.0,
     'g_post_mix': 8.0,
     'g_pre_ffn': 21.473,
     'g_post_ffn': 34.071}
    for name, (base, spread) in spreads.items():
        noise = np.random.default_rng([zlib.crc32(name.encode()), seed]).standard_normal(out[name].shape)
        drawn = base * np.exp(spread * noise) if base else spread * noise
        out[name] = __import__('jax').numpy.asarray(drawn.astype(out[name].dtype))
    for name, factor in factors.items():
        out[name] = (out[name] * factor).astype(out[name].dtype)
    return out
```

```python
from contextlib import ExitStack

import concourse.bass as bass
from concourse import mybir

F32 = mybir.dt.float32
F32R = mybir.dt.float32r
I32 = mybir.dt.int32

ACT = mybir.ActivationFunctionType
ALU = mybir.AluOpType
AX = mybir.AxisListType

P = 128
TT = 2
T = TT * P
D = 2048
KD = D // P
NW = 512
KC = 2
GD = D // NW
CD = KD // KC
HPG = NW // P
NG = D // NW
ROPE = 64
HR = ROPE // 2
LORA = 512
CL = LORA // P // KC
CR = NW // P // KC
D_FF = 5632
NF = D_FF // NW
N_MOD = 6
EPS = 1e-6
SCALE = float(P + ROPE) ** -0.5
RING = 4
AHEAD = RING - 1
LEVELS = [64, 32, 16, 8, 4, 2, 1]
ADA_A = 3
TWO_PI_HI, TWO_PI_MID = 6.28125, 0.00193500518798828125
TWO_PI_LO = 6.283185307179586 - TWO_PI_HI - TWO_PI_MID
ROUND = 12582912.0

C_C, C_BADA = 0, KD
C_GPRE, C_GPOST, C_GPRE2, C_GPOST2 = (C_BADA + N_MOD * KD + KD * i for i in range(4))
C_GQ = C_GPOST2 + KD
C_GKV = C_GQ + LORA // P
C_LB = C_GKV + LORA // P
C_END = C_LB + 2 * KD
K_ID, K_NEG, K_ONE, K_GHG, K_FREQ = 0, P, 2 * P, 3 * P, 4 * P
K_POW = K_FREQ + HR
K_END = K_POW + TT * HPG
SH_M, SC_M, GA_M, SH_F, SC_F, GA_F = (i * KD for i in range(N_MOD))


class Place:

    def __init__(self, chunk, group, chunks=0, groups=0, i=0):
        self.chunk, self.group, self.chunks, self.groups, self.i = chunk, group, chunks, groups, i

    def slot(self, c):
        return (self.chunk + c) % RING

    def turn(self, c):
        return (self.chunk + c) // RING + self.i * (self.chunks // RING)

    def through(self, c):
        return self.i * self.chunks + (self.chunk + c + 1)

    def pair(self, g):
        return (self.group + g) % 2

    def starts(self, c):
        return self.chunks == 0 and self.chunk + c < RING

    def fresh(self, g):
        return self.groups == 0 and self.group + g < 2

    def freed(self, g):
        return self.i * (self.groups // 2) + (self.group + g) // 2


def build(nc, x, vectors, consts, masks, positions, ada0, ada1, w_c, w_kr, w_uqn, w_uqr, w_uk, w_uv, w_hf,
          w_hq, w_hi, w_hg, w_omla, w_ohg, w_ga, w_gb, w_out, w_gate, w_up, w_down, out):
    ctx = ExitStack()
    with ctx:
        def sb(name, shape, dt=F32):
            return ctx.enter_context(nc.sbuf_tensor(name, shape, dt))

        raw = sb("raw", [P, RING, KC * NW])
        whi = sb("whi", [P, RING, KC * NW], F32R)
        wlo = sb("wlo", [P, RING, KC * NW], F32R)
        ada_raw = sb("ada_raw", [P, 2, KC * NW])
        ada_acc = sb("ada_acc", [P, 2, NW])
        hT_hi = sb("hT_hi", [P, KD, T], F32R)
        hT_lo = sb("hT_lo", [P, KD, T], F32R)
        cT_hi = sb("cT_hi", [P, 2, LORA // P, T], F32R)
        cT_lo = sb("cT_lo", [P, 2, LORA // P, T], F32R)
        ya = sb("ya", [P, TT, D])
        yb = sb("yb", [P, TT, D])
        stage = sb("stage", [P, TT, NW])
        side = sb("side", [P, TT, NW])
        qT = sb("qT", [P, 2 * HPG, P])
        kT = sb("kT", [P, 2 * HPG, P])
        bT = sb("bT", [P, 2 * HPG, P])
        dec = sb("dec", [P, 2, 2 * HPG * P])
        zT = sb("zT", [P, 2, 2 * HPG * P])
        pT = sb("pT", [P, 2 * HPG, P])
        pTx = sb("pTx", [P, HPG, P])
        v = sb("v", [P, TT, NW])
        attT_hi = sb("attT_hi", [P, HPG, T], F32R)
        attT_lo = sb("attT_lo", [P, HPG, T], F32R)
        oT_hi = sb("oT_hi", [P, HPG, T], F32R)
        oT_lo = sb("oT_lo", [P, HPG, T], F32R)
        vec = sb("vec", [P, C_END])
        con = sb("con", [P, K_END])
        msk = sb("msk", [P, len(LEVELS) * 64 + P], I32)
        pos = sb("pos", [P, TT], I32)
        posf = sb("posf", [P, TT])
        mods = sb("mods", [P, N_MOD * KD])
        scale_h = sb("scale_h", [P, KD])
        gain_y = sb("gain_y", [P, KD])
        lb = sb("lb", [P, 4, KD])
        csilu = sb("csilu", [P, KD])
        cos = sb("cos", [P, TT, HR])
        sin = sb("sin", [P, TT, HR])
        krT = sb("krT", [ROPE, T])
        stat = sb("stat", [P, 40])
        sums = sb("sums", [P, TT, GD])
        ident = con[:, K_ID:K_ID + P]
        ones = con[:, K_ONE:K_ONE + P]

        PS = ctx.enter_context(nc.psum_tensor("PS", [P, 8, NW], F32))
        XA, XB = 4, 6

        xT = yb[:].rearrange("p a (b c) -> p (a b) c", c=NW)
        prob = dec[:].rearrange("p a b -> p (a b)")[:, 0:3 * NW].rearrange("p (h j s) -> p h j s", h=HPG, j=3)
        rotated = zT[:, 1, 0:NW].rearrange("p (t h d) -> p t h d", t=TT, h=HPG)
        by_rms = stage[:].rearrange("p t c -> p (t c)")[:, 0:TT * P].rearrange("p (t c) -> p t c", t=TT)
        gain_row = zT[:].rearrange("p a b -> p (a b)")
        all_dec = dec[:].rearrange("p a b -> p (a b)")

        def diagonal(k):
            return (qT, kT)[k // (2 * HPG)][:, k % (2 * HPG)]

        def banks(b):
            return PS[:, b:b + 2, :]

        def by_tile(b):
            return PS[:, b:b + 2, :].rearrange("p b (i s) -> p (b i) s", s=P)

        def by_ktile(b):
            return PS[:, b:b + 2, :].rearrange("p b (k t) -> p (b k) t", t=T)

        def flat_banks(b):
            return PS[:, b:b + 2, :].rearrange("p b c -> p (b c)")

        def gates(j):
            return dec[:, j, :].rearrange("p (t c) -> p t c", t=TT)

        def pairs(t, kp):
            return t[:, 2 * kp:2 * kp + 2, :].rearrange("p k t -> p (k t)")

        def flat(t):
            return t[:].rearrange("p i s -> p (i s)")

        def tiles(f):
            return f.rearrange("p (h two s) -> p h two s", two=2, s=P)

        def halves(f, m):
            return f.rearrange("p (x two m) -> p x two m", two=2, m=m)

        sems = {}

        def sig(name):
            if name not in sems:
                sems[name] = ctx.enter_context(nc.semaphore(name))
            return sems[name]

        raw_loaded = [sig(f"raw_loaded{s}") for s in range(RING)]
        ada_loaded = [sig(f"ada_loaded{s}") for s in range(2)]
        pair_free = [sig("pair_free0"), sig("pair_free1")]
        hi_ready, lo_ready, multiplied = sig("hi_ready"), sig("lo_ready"), sig("multiplied")

        ADA0 = 2 * GD * CD
        ADA_TURNS = ADA0 // RING
        ADA_STEPS = 2 * GD * KD

        def freed_by(p, groups):
            return (groups - p + 1) // 2

        N_C = 3 * CD
        A_UQ, A_UK, A_UR, A_UV = 0, CL, 2 * CL, 3 * CL
        A_HF = 4 * CL
        A_HQ, A_HI, A_HG = A_HF + CD, A_HF + 2 * CD, A_HF + 3 * CD
        A_OM = A_HF + 4 * CD
        A_OH = A_OM + GD * CR
        A_N = A_OH + GD * CR
        AG = 8 + 2 * GD
        B_GATE = N_C + NG * A_N
        G_GATE = 3 + NG * AG
        B_OUT, G_OUT = B_GATE + GD * 2 * CD, G_GATE + 2 * GD
        B_FF, G_FF = B_OUT + GD * CD, G_OUT + GD
        F_N = 2 * CD + GD * CR
        B_FF1, G_FF1 = B_FF + 2 * CD, G_FF + 2
        B_LAST, G_LAST = B_FF1 + (NF - 1) * F_N, G_FF1 + (NF - 1) * (2 + GD)

        def place_c():
            return Place(0, 0)

        def place_a(g):
            return Place(N_C, 3, A_N, AG, g)

        def place_gate(n):
            return Place(B_GATE, G_GATE, 2 * CD, 2, n)

        def place_out(n):
            return Place(B_OUT, G_OUT, 2 * CD, 2, n)

        def place_ff(n):
            return Place(B_FF1 - F_N, G_FF1 - (2 + GD), F_N, 2 + GD, n)

        ADA_GATE = NG * ADA_A
        ada_step = sig("ada_step")
        A_ADA, G_ADA = 3, 4
        LEAD = 2

        block = ctx.enter_context(nc.Block())

        @block.sync
        def _(sp):
            sp.dma_start(vec[:], vectors).then_inc(sig("vectors_loaded"), 16)
            sp.dma_start(pos[:], positions).then_inc(sig("positions_loaded"), 16)
            sp.dma_start(con[:], consts).then_inc(sig("constants_loaded"), 16)
            sp.dma_start(ya[:], x).then_inc(sig("x_loaded"), 16)
            sp.dma_start(msk[:], masks).then_inc(sig("masks_loaded"), 16)

            for c in range(RING):
                sp.dma_start(raw[:, c], ada0[c]).then_inc(raw_loaded[c], 16)
            with sp.Fori(0, ADA_TURNS - 1) as i:
                for c in range(RING):
                    sp.wait_ge(ada_step, i * (RING * KC) + (c + 1) * KC)
                    sp.dma_start(raw[:, c], ada0[(i + 1) * RING + c]).then_inc(raw_loaded[c], 16)

            def load(pl, c, src, width=NW):
                if pl.starts(c):
                    sp.wait_ge(ada_step, (ADA0 - RING + c + 1) * KC)
                else:
                    sp.wait_ge(lo_ready, pl.through(c) - RING)
                sp.dma_start(raw[:, pl.slot(c), 0:KC * width], src).then_inc(raw_loaded[pl.slot(c)], 16)

            def load_ada(group, a):
                sp.wait_ge(ada_step, group * KD + (ADA_STEPS + (a - 1) * KC))
                sp.dma_start(ada_raw[:, a % 2], ada1[group * CD + a]).then_inc(ada_loaded[a % 2], 16)

            pl = place_c()
            for c in range(2 * CD):
                load(pl, c, w_c[c])
            for c in range(CD):
                load(pl, 2 * CD + c, w_kr[c], ROPE)
            with sp.Fori(0, NG) as g:
                pl = place_a(g)
                stream = [(w[g, c], NW) for w in (w_uqn, w_uk) for c in range(CL)]
                stream += [(w_uqr[g, c], NW // 2) for c in range(CL)] + [(w_uv[g, c], NW) for c in range(CL)]
                stream += [(w[g, c], NW) for w in (w_hf, w_hq, w_hi, w_hg) for c in range(CD)]
                stream += [(w[g, n, c], NW) for w in (w_omla, w_ohg) for n in range(GD) for c in range(CR)]
                for c, (src, width) in enumerate(stream):
                    load(pl, c, src, width)
                    a = c - A_ADA - LEAD
                    if 0 <= a < ADA_A * CD:
                        load_ada(g * ADA_A + a // CD, a % CD)
            with sp.Fori(0, GD) as n:
                pl = place_gate(n)
                for c in range(2 * CD):
                    load(pl, c, (w_ga if c < CD else w_gb)[n, c % CD])
                    a = c - G_ADA - LEAD
                    if 0 <= a < CD:
                        load_ada(n + ADA_GATE, a)
            with sp.Fori(0, GD // 2) as n:
                pl = place_out(n)
                for c in range(2 * CD):
                    load(pl, c, w_out[n * 2 + c // CD, c % CD])
            sp.wait_ge(sig("gated"), GD)
            sp.dma_start(yb[:], x).then_inc(sig("x_again"), 16)
            first = Place(B_FF, G_FF)
            for c in range(2 * CD):
                load(first, c, (w_gate if c < CD else w_up)[0, c % CD])
            with sp.Fori(1, NF) as n:
                pl = place_ff(n)
                for c in range(CD):
                    load(pl, c, w_gate[n, c])
                for c in range(GD * CR):
                    load(pl, CD + c, w_down[n - 1, c // CR, c % CR])
                for c in range(CD):
                    load(pl, CD + GD * CR + c, w_up[n, c])
            pl = Place(B_LAST, G_LAST)
            for c in range(GD * CR):
                load(pl, c, w_down[NF - 1, c // CR, c % CR])
            for n in range(GD):
                sp.wait_ge(sig("x_final"), TT * (n + 1))
                sp.dma_start(out[:, :, n * NW:(n + 1) * NW], yb[:, :, n * NW:(n + 1) * NW])\
                  .then_inc(sig("stored"), 16)
            sp.wait_ge(sig("stored"), 16 * GD)

        @block.scalar
        def _(act):
            def high(pl, c, width=NW):
                act.wait_ge(raw_loaded[pl.slot(c)], (pl.turn(c) + ADA_TURNS + 1) * 16)
                if not pl.starts(c):
                    act.wait_ge(multiplied, pl.through(c) - RING)
                w = KC * width
                nc.scalar.activation(whi[:, pl.slot(c), 0:w], raw[:, pl.slot(c), 0:w], ACT.Copy)\
                  .then_inc(hi_ready, 1)

            def from_pair(pl, g, c, dst, func=ACT.Copy, free=True, done=None):
                act.wait_ge(multiplied, pl.through(c))
                p = pl.pair(g)
                i = nc.scalar.activation(dst, banks(2 * p), func)
                i.then_inc(pair_free[p] if free else sig(done), 1)

            def square_sum(src, junk, to):
                return nc.scalar.activation(junk, src, ACT.Square, accum_out=to)

            act.wait_ge(sig("vectors_loaded"), 16)
            nc.scalar.activation(csilu[:], vec[:, C_C:C_C + KD], ACT.Sigmoid).then_inc(sig("c_sigmoid"), 1)
            act.wait_ge(sig("x_loaded"), 16)
            for tt in range(TT):
                if tt:
                    act.wait_ge(sig("x_squared"), tt)
                square_sum(ya[:, tt], all_dec, stat[:, tt:tt + 1]).then_inc(sig("x_squared"), 1)
            act.wait_ge(sig("lb_centred"), 2)
            nc.scalar.activation(lb[:, 1:3], lb[:, 1:3], ACT.Exp).then_inc(sig("lb_exp"), 1)
            act.wait_ge(sig("angle_ready"), 1)
            nc.scalar.activation(sin[:].rearrange("p t f -> p (t f)"), stage[:, 0, 0:TT * HR], ACT.Sin).then_inc(sig("sin_ready"), 1)
            nc.scalar.activation(cos[:].rearrange("p t f -> p (t f)"), stage[:, 0, 0:TT * HR], ACT.Sin, scale=0.5).then_inc(sig("sin_ready"), 1)
            for kp in range(KD // 2):
                act.wait_ge(sig("x_transposed"), kp + 1)
                nc.scalar.activation(xT[:, kp], PS[:, kp % 4, :], ACT.Copy).then_inc(sig("xT_copied"), 1)
            for kp in range(KD // 2):
                act.wait_ge(sig("h_scaled"), kp + 1)
                nc.scalar.activation(pairs(hT_hi, kp), xT[:, kp], ACT.Copy)\
                  .then_inc(sig("h_high"), 1)

            pl = place_c()
            for c in range(CD + 3):
                high(pl, c)
            for j, (dst, c_next) in enumerate(((stage, 2 * CD + 3), (side, 3 * CD + AHEAD))):
                from_pair(pl, j, (j + 1) * CD - 1, dst[:])
                act.wait_ge(pair_free[j], 1)
                for tt in range(TT):
                    if tt or j:
                        act.wait_ge(sig("c_squared"), 2 * j + tt)
                    square_sum(dst[:, tt], dec[:, 0, 0:NW], stat[:, 4 + 2 * j + tt:5 + 2 * j + tt])\
                        .then_inc(sig("c_squared"), 1)
                for c in range((j + 1) * CD + 3, c_next):
                    high(pl, c, ROPE if 2 * CD <= c < 3 * CD else NW)
                act.wait_ge(sig("c_scaled"), 4 * (j + 1))
                nc.scalar.activation(cT_hi[:, j].rearrange("p k t -> p (k t)"), zT[:, j, :], ACT.Copy).then_inc(sig("c_high"), 1)
            act.wait_ge(sig("kr_transposed"), 1)
            nc.scalar.activation(krT[:], PS[0:ROPE, XA, 0:T], ACT.Copy).then_inc(sig("krT_copied"), 1)

            with act.Fori(0, NG) as g:
                pl = place_a(g)

                def highs(a, b):
                    for c in range(a, b):
                        high(pl, c, NW // 2 if A_UR <= c < A_UV else NW)

                highs(AHEAD, 5)
                from_pair(pl, 0, A_UK - 1, stage[:])
                highs(5, 7)
                from_pair(pl, 1, A_UR - 1, side[:])
                highs(7, 9)
                act.wait_ge(sig("q_transposed"), g + 1)
                nc.scalar.activation(qT[:], by_tile(XA), ACT.Copy).then_inc(sig("qT_copied"), 1)
                highs(9, 11)
                from_pair(pl, 3, 7, v[:])
                highs(11, 12)
                act.wait_ge(sig("k_transposed"), g + 1)
                nc.scalar.activation(kT[:], by_tile(XB), ACT.Copy).then_inc(sig("kT_copied"), 1)
                highs(12, 13)
                act.wait_ge(sig("qr_transposed"), g + 1)
                nc.scalar.activation(bT[0:ROPE], by_tile(XA)[0:ROPE], ACT.Copy)\
                  .then_inc(sig("qrT_copied"), 1)
                highs(13, 15)
                act.wait_ge(sig("scored"), g + 1)
                nc.scalar.activation(prob[:, :, 1, :], by_tile(XB)[:, 0:HPG], ACT.Copy).then_inc(sig("scores_copied"), 1)
                highs(15, 17)
                act.wait_ge(sig("max_ready"), g + 1)
                for h in range(HPG):
                    for tt in range(TT):
                        cols = prob[:, h, tt:1 + 2 * tt, :]
                        at = tt * HPG + h
                        nc.scalar.activation(cols, cols, ACT.Exp, bias=stat[:, 16 + at:17 + at], scale=SCALE,
                                             accum_out=stat[:, 24 + at:25 + at]).then_inc(sig("exps"), 1)
                highs(17, 20)
                act.wait_ge(sig("p_transposed"), g + 1)
                nc.scalar.activation(pT[:], by_tile(XA), ACT.Copy).then_inc(sig("p_copied"), 1)
                nc.scalar.activation(pTx[:], by_tile(XB)[:, 0:HPG], ACT.Copy).then_inc(sig("p_copied"), 1)
                from_pair(pl, 4, A_HF + CD - 1, stage[:])
                highs(20, 25)
                act.wait_ge(sig("att_transposed"), g + 1)
                nc.scalar.activation(attT_hi[:], by_ktile(XA), ACT.Copy).then_inc(sig("att_high"), 1)
                highs(25, 26)
                act.wait_ge(sig("hf_transposed"), g + 1)
                nc.scalar.activation(kT[:], by_tile(XB), ACT.Sigmoid).then_inc(sig("f_sigmoid"), 1)
                highs(26, 27)
                from_pair(pl, 5, A_HQ + CD - 1, side[:])
                highs(27, 29)
                act.wait_ge(sig("hq_transposed"), g + 1)
                nc.scalar.activation(qT[:], by_tile(XA), ACT.Sigmoid).then_inc(sig("q_sigmoid"), 1)
                act.wait_ge(sig("f_ready"), g * HPG + HPG)
                nc.scalar.activation(bT[:], kT[:], ACT.Ln).then_inc(sig("log_f"), 1)
                highs(29, 31)
                for L in range(len(LEVELS) + 1):
                    highs(31 + 2 * L, 32 + 2 * L)
                    if L == len(LEVELS):
                        act.wait_ge(sig("b_ready"), g * 8 + 8)
                        nc.scalar.activation(tiles(dec[:, L % 2])[:, :, 1, :], tiles(flat(bT))[:, :, 1, :], ACT.Exp)\
                          .then_inc(sig("decays"), 1)
                        act.wait_ge(sig("diffs"), g * 8 + (L + 1))
                        dif = tiles(dec[:, L % 2])[:, :, 0, :]
                    else:
                        act.wait_ge(sig("diffs"), g * 8 + (L + 1))
                        dif = dec[:, L % 2]
                    nc.scalar.activation(dif, dif, ACT.Exp).then_inc(sig("decays"), 1)
                    highs(32 + 2 * L, 33 + 2 * L)
                    if 32 + 2 * L == 34:
                        from_pair(pl, 6, A_HI + CD - 1, v[:])
                    if 32 + 2 * L == 42:
                        from_pair(pl, 7, A_HG + CD - 1, side[:], ACT.Sigmoid, False, "og_sigmoid")
                highs(47, 48)
                act.wait_ge(sig("cross_scored"), g + 1)
                nc.scalar.activation(pTx[:], by_tile(XB)[:, HPG:], ACT.Copy).then_inc(sig("cross_copied"), 1)
                highs(48, 49)
                act.wait_ge(sig("o_summed"), g + 1)
                nc.scalar.activation(dec[:, 0, :], flat_banks(XB), ACT.Square).then_inc(sig("o_squared"), 1)
                highs(49, 51)
                act.wait_ge(sig("o_transposed"), g + 1)
                nc.scalar.activation(oT_hi[:], by_ktile(XA), ACT.Copy).then_inc(sig("o_high"), 1)
                highs(51, A_N + AHEAD)

            with act.Fori(0, GD) as n:
                pl = place_gate(n)
                for c in range(AHEAD, CD + 3):
                    high(pl, c)
                from_pair(pl, 0, CD - 1, gates(0), ACT.Sigmoid)
                for c in range(CD + 3, 2 * CD + AHEAD):
                    high(pl, c)
                from_pair(pl, 1, 2 * CD - 1, gates(1), ACT.Sigmoid)

            act.wait_ge(sig("gain_spread"), 1)
            for i in range(2):
                nc.scalar.activation(zT[:, i], flat_banks(XA + 2 * i), ACT.Copy).then_inc(sig("gain_copied"), 1)
            for kp in range(KD // 2):
                act.wait_ge(sig("m_transposed"), kp + 1)
                nc.scalar.activation(pairs(hT_hi, kp), PS[:, XA + kp % 4, :], ACT.Copy)\
                  .then_inc(sig("m_high"), 1)

            with act.Fori(0, GD // 2) as n:
                pl = place_out(n)
                for j in range(2):
                    for c in range(j * CD + AHEAD, (j + 1) * CD + AHEAD):
                        high(pl, c)
                    act.wait_ge(multiplied, pl.through((j + 1) * CD - 1))
                    for tt in range(TT):
                        if j or tt:
                            act.wait_ge(sig("y_squared"), n * (2 * TT) + (j * TT + tt))
                        nc.scalar.activation(dec[:, 0, 0:NW], PS[:, 2 * pl.pair(j) + tt, :], ACT.Square,
                                             accum_out=sums[:, tt, bass.ds(n * 2 + j, 1)])\
                          .then_inc(sig("y_squared"), 1)
            for tt in range(TT):
                act.wait_ge(sig("x_mixed"), tt + 1)
                if tt:
                    act.wait_ge(sig("x2_squared"), tt)
                square_sum(yb[:, tt], all_dec, stat[:, 10 + tt:11 + tt]).then_inc(sig("x2_squared"), 1)
            for kp in range(KD // 2):
                act.wait_ge(sig("h2_scaled"), 2 * kp + 2)
                nc.scalar.activation(pairs(hT_hi, kp), dec[:, kp % 2, 0:NW], ACT.Copy)\
                  .then_inc(sig("h2_high"), 1)

            def hidden_high(n):
                act.wait_ge(sig("ff_transposed"), n)
                nc.scalar.activation(oT_hi[:], by_ktile(XA), ACT.Copy).then_inc(sig("ff_high"), 1)

            first = Place(B_FF, G_FF)
            for c in range(AHEAD, CD + 3):
                high(first, c)
            from_pair(first, 0, CD - 1, stage[:], ACT.Sigmoid, False, "ff_sigmoid")
            for c in range(CD + 3, 2 * CD):
                high(first, c)
            with act.Fori(1, NF) as n:
                pl = place_ff(n)
                for c in range(7):
                    high(pl, c)
                hidden_high(n)
                for c in range(7, CD + 3):
                    high(pl, c)
                from_pair(pl, 0, CD - 1, stage[:], ACT.Sigmoid, False, "ff_sigmoid")
                for c in range(CD + 3, F_N):
                    high(pl, c)
            pl = Place(B_LAST, G_LAST)
            for c in range(RING):
                high(pl, c)
            hidden_high(NF)
            for c in range(RING, GD * CR):
                high(pl, c)
            for n in range(GD):
                p = (G_LAST + n) % 2
                act.wait_ge(pair_free[p], freed_by(p, G_LAST + n + 1))
                for tt in range(TT):
                    if n or tt:
                        act.wait_ge(sig("y2_squared"), n * TT + tt)
                    square_sum(ya[:, tt, n * NW:(n + 1) * NW], dec[:, 0, 0:NW], sums[:, tt, n:n + 1])\
                        .then_inc(sig("y2_squared"), 1)

        @block.gpsimd
        def _(pool):
            def power(src, width, name, count=0):
                pool.wait_ge(sig(name + "_mean"), count + 1)
                nc.gpsimd.tensor_tensor(src, src, con[:, K_POW:K_POW + width], ALU.pow)\
                  .then_inc(sig(name + "_rsqrt"), 1)

            pool.wait_ge(sig("constants_loaded"), 16)
            power(stat[:, 0:TT], TT, "trunk")
            pool.wait_ge(sig("x_transposed"), KD // 2)
            nc.gpsimd.memset(ya[:], 0.0).then_inc(sig("sums_zeroed"), 1)
            for j in range(2):
                power(stat[:, 4 + 2 * j:6 + 2 * j], TT, "c", j)
                if j == 0:
                    pool.wait_ge(sig("h_low"), KD // 2)
                    nc.gpsimd.memset(yb[:], 0.0).then_inc(sig("sums_zeroed"), 1)
            with pool.Fori(0, NG) as g:
                power(stat[:, 32:40], TT * HPG, "o", g)
            power(stat[:, 8:8 + TT], TT, "trunk", 1)
            power(stat[:, 10:10 + TT], TT, "trunk", 2)
            power(stat[:, 12:12 + TT], TT, "trunk", 3)

        @block.tensor
        def _(pe):
            def multiply(pl, g, n, c0, a, b, hi, lo, width=NW, kt0=0):
                p = pl.pair(g)
                for c in range(a, b):
                    if c == 0 and not pl.fresh(g):
                        pe.wait_ge(pair_free[p], pl.freed(g))
                    pe.wait_ge(lo_ready, pl.through(c0 + c))
                    s = pl.slot(c0 + c)
                    for tt in range(TT):
                        for k in range(KC):
                            kt = kt0 + c * KC + k
                            tok = slice(tt * P, (tt + 1) * P)
                            cols = slice(k * width, (k + 1) * width)
                            o = PS[:, 2 * p + tt, 0:width]
                            start, stop = c == 0 and k == 0, c == n - 1 and k == KC - 1
                            nc.tensor.matmul(o, hi[:, kt, tok], whi[:, s, cols], start=start, stop=False)
                            nc.tensor.matmul(o, hi[:, kt, tok], wlo[:, s, cols], start=False, stop=False)
                            last = nc.tensor.matmul(o, lo[:, kt, tok], whi[:, s, cols], start=False, stop=stop)
                    last.then_inc(multiplied, 1)

            def transpose_group(src, bank):
                for h in range(HPG):
                    for tt in range(TT):
                        last = nc.tensor.transpose(PS[:, bank + h // 2, ((h % 2) * TT + tt) * P:][:, 0:P],
                                                   src[:, tt, h * P:(h + 1) * P], ident)
                return last

            def transpose_pair(src, kp, bank):
                for j in range(2):
                    for tt in range(TT):
                        k = 2 * kp + j
                        last = nc.tensor.transpose(PS[:, bank, (j * TT + tt) * P:][:, 0:P],
                                                   src[:, tt, k * P:(k + 1) * P], ident)
                return last

            def attend():
                for h in range(HPG):
                    cols = slice(h * P, (h + 1) * P)
                    nc.tensor.matmul(PS[:, XB, cols], pT[:, 2 * h], v[:, 0, cols], start=True, stop=True)
                    nc.tensor.matmul(PS[:, XB + 1, cols], pTx[:, h], v[:, 0, cols], start=True, stop=False)
                    last = nc.tensor.matmul(PS[:, XB + 1, cols], pT[:, 2 * h + 1], v[:, 1, cols],
                                            start=False, stop=True)
                return last

            def sum_rows(acc, bank, at=0):
                for j in range(NW // P):
                    last = nc.tensor.matmul(PS[:, bank, at + j:at + j + 1], acc[:, j * P:(j + 1) * P], ones[:, 0:1],
                                            start=True, stop=True)
                return last

            pe.wait_ge(sig("constants_loaded"), 16)
            pe.wait_ge(sig("x_scaled"), TT)
            for kp in range(KD // 2):
                if kp >= 4:
                    pe.wait_ge(sig("xT_copied"), kp - 3)
                transpose_pair(ya, kp, kp % 4).then_inc(sig("x_transposed"), 1)
            for q in range(2 * GD):
                pe.wait_ge(ada_step, KD * (q + 1))
                sum_rows(ada_acc[:, q % 2], XA, q * (NW // P)).then_inc(sig(f"ada0_summed{q % 2}"), 1)

            pl = place_c()
            pe.wait_ge(sig("h_low"), KD // 2)
            multiply(pl, 0, CD, 0, 0, CD, hT_hi, hT_lo)
            multiply(pl, 1, CD, CD, 0, 2, hT_hi, hT_lo)
            for j in range(2):
                if j == 0:
                    multiply(pl, 1, CD, CD, 2, CD, hT_hi, hT_lo)
                else:
                    multiply(pl, 2, CD, 2 * CD, 0, CD, hT_hi, hT_lo, ROPE)
                pe.wait_ge(sig("c_normed"), TT * (j + 1))
                if j:
                    pe.wait_ge(sig("c_scaled"), 4)
                transpose_group(stage if j == 0 else side, XA).then_inc(sig("c_transposed"), 1)
            pe.wait_ge(sig("kr_rotated"), 1)
            pe.wait_ge(sig("c_scaled"), 8)
            for tt in range(TT):
                last = nc.tensor.transpose(PS[0:ROPE, XA, tt * P:(tt + 1) * P],
                                           qT[:, tt, 0:ROPE], ident)
            last.then_inc(sig("kr_transposed"), 1)
            pe.wait_ge(sig("c_low"), 2)
            pe.wait_ge(sig("krT_copied"), 1)

            with pe.Fori(0, NG) as g:
                pl = place_a(g)

                def hf(a, b):
                    multiply(pl, 4, CD, A_HF, a - A_HF, b - A_HF, hT_hi, hT_lo)

                def hq(a, b):
                    multiply(pl, 5, CD, A_HQ, a - A_HQ, b - A_HQ, hT_hi, hT_lo)

                def after_hq(c):
                    if c < A_HG:
                        multiply(pl, 6, CD, A_HI, c - A_HI, c + 1 - A_HI, hT_hi, hT_lo)
                    elif c < A_OM:
                        multiply(pl, 7, CD, A_HG, c - A_HG, c + 1 - A_HG, hT_hi, hT_lo)
                    else:
                        n, k = (c - A_OM) // CR, (c - A_OM) % CR
                        multiply(pl, 8 + n, CR, A_OM + n * CR, k, k + 1, attT_hi, attT_lo)

                multiply(pl, 0, CL, A_UQ, 0, CL, cT_hi[:, 0], cT_lo[:, 0])
                multiply(pl, 1, CL, A_UK, 0, CL, cT_hi[:, 1], cT_lo[:, 1])
                multiply(pl, 2, CL, A_UR, 0, CL, cT_hi[:, 0], cT_lo[:, 0], NW // 2)
                pe.wait_ge(pair_free[pl.pair(0)], pl.freed(0) + 1)
                transpose_group(stage, XA).then_inc(sig("q_transposed"), 1)
                multiply(pl, 3, CL, A_UV, 0, CL, cT_hi[:, 1], cT_lo[:, 1])
                hf(8, 9)
                pe.wait_ge(pair_free[pl.pair(1)], pl.freed(1) + 1)
                transpose_group(side, XB).then_inc(sig("k_transposed"), 1)
                pe.wait_ge(sig("qT_copied"), g + 1)
                hf(9, 10)
                pe.wait_ge(sig("constants_loaded"), 16)
                pe.wait_ge(sig("qr_rotated"), g + 1)
                for h in range(HPG):
                    for tt in range(TT):
                        last = nc.tensor.transpose(PS[0:ROPE, XA + h // 2, ((h % 2) * TT + tt) * P:][:, 0:P],
                                                   rotated[:, tt, h, :], ident)
                last.then_inc(sig("qr_transposed"), 1)
                hf(10, 12)
                pe.wait_ge(sig("kT_copied"), g + 1)
                pe.wait_ge(sig("qrT_copied"), g + 1)
                for h in range(HPG):
                    for tt, s, o in ((0, 0, PS[:, XA + h // 2, (h % 2) * 2 * P:][:, 0:P]),
                                     (1, 1, PS[:, XA + h // 2, (h % 2) * 2 * P + P:][:, 0:P]),
                                     (1, 0, PS[:, XB, h * P:(h + 1) * P])):
                        nc.tensor.matmul(o, qT[:, 2 * h + tt], kT[:, 2 * h + s], start=True, stop=False)
                        last = nc.tensor.matmul(o, bT[0:ROPE, 2 * h + tt], krT[:, s * P:(s + 1) * P],
                                                start=False, stop=True)
                last.then_inc(sig("scored"), 1)
                pe.wait_ge(ada_step, g * (ADA_A * KD) + (ADA_STEPS + KD))
                sum_rows(ada_acc[:, 0], XB + 1).then_inc(sig("ada_summed_a"), 1)
                hf(12, 16)
                hq(16, 17)
                pe.wait_ge(sig("exps"), g * 8 + 8)
                for h in range(HPG):
                    for tt in range(TT):
                        nc.tensor.transpose(PS[:, XA + h // 2, ((h % 2) * TT + tt) * P:][:, 0:P],
                                            prob[:, h, 2 * tt, :], ident)
                    last = nc.tensor.transpose(PS[:, XB, h * P:(h + 1) * P], prob[:, h, 1, :], ident)
                last.then_inc(sig("p_transposed"), 1)
                hq(17, 20)
                pe.wait_ge(sig("p_copied"), g * 2 + 2)
                pe.wait_ge(sig("mods_a"), g + 1)
                attend().then_inc(sig("att_summed"), 1)
                pe.wait_ge(ada_step, g * (ADA_A * KD) + (ADA_STEPS + 2 * KD))
                sum_rows(ada_acc[:, 1], XA).then_inc(sig("ada_summed_b"), 1)
                hq(20, 22)
                pe.wait_ge(sig("mods_b"), g + 1)
                pe.wait_ge(sig("att_scaled"), g + 1)
                transpose_group(side, XA).then_inc(sig("att_transposed"), 1)
                hq(22, 23)
                pe.wait_ge(pair_free[pl.pair(4)], pl.freed(4) + 1)
                transpose_group(stage, XB).then_inc(sig("hf_transposed"), 1)
                hq(23, 24)
                after_hq(24)
                after_hq(25)
                pe.wait_ge(sig("att_low"), g + 1)
                pe.wait_ge(pair_free[pl.pair(5)], pl.freed(5) + 1)
                transpose_group(side, XA).then_inc(sig("hq_transposed"), 1)
                for c in range(26, 30):
                    after_hq(c)
                pe.wait_ge(sig("q_ready"), g + 1)
                pe.wait_ge(sig("k_ready"), g + 1)
                for i in range(2 * HPG):
                    last = nc.tensor.matmul(PS[:, XB + i // 4, (i % 4) * P:][:, 0:P], kT[:, i], qT[:, i],
                                            start=True, stop=True)
                last.then_inc(sig("self_scored"), 1)
                for L, m in enumerate(LEVELS):
                    after_hq(30 + 2 * L)
                    pe.wait_ge(sig("decayed"), g * 8 + (L + 1))
                    if L >= 2:
                        pe.wait_ge(sig("self_merged"), g + 1)
                    if L >= 4:
                        pe.wait_ge(sig(f"level{L - 4}_merged"), g + 1)
                    z = zT[:, L % 2].rearrange("p (i s) -> p i s", s=P)
                    zt = zT[:, L % 2].rearrange("p (i x two m) -> p i x two m", i=2 * HPG, two=2, m=m)
                    for i in range(2 * HPG):
                        last = nc.tensor.matmul(PS[:, XA + L % 4, i * 64:(i + 1) * 64], z[:, i],
                                                zt[:, i, :, 1, :], start=True, stop=True)
                    last.then_inc(sig(f"level{L}_scored"), 1)
                    after_hq(31 + 2 * L)
                after_hq(44)
                L = len(LEVELS)
                pe.wait_ge(sig("decayed"), g * 8 + (L + 1))
                pe.wait_ge(sig(f"level{L - 4}_merged"), g + 1)
                for h in range(HPG):
                    z = zT[:, L % 2].rearrange("p (i s) -> p i s", s=P)
                    last = nc.tensor.matmul(PS[:, XB + 1, h * P:(h + 1) * P], z[:, 2 * h], z[:, 2 * h + 1],
                                            start=True, stop=True)
                last.then_inc(sig("cross_scored"), 1)
                after_hq(45)
                pe.wait_ge(sig(f"level{len(LEVELS) - 1}_merged"), g + 1)
                pe.wait_ge(sig("cross_copied"), g + 1)
                attend().then_inc(sig("o_summed"), 1)
                after_hq(46)
                after_hq(47)
                pe.wait_ge(sig("o_gated"), g + 1)
                transpose_group(stage, XA).then_inc(sig("o_transposed"), 1)
                pe.wait_ge(ada_step, g * (ADA_A * KD) + (ADA_STEPS + 3 * KD))
                sum_rows(ada_acc[:, 0], XB + 1).then_inc(sig("ada_summed_c"), 1)
                pe.wait_ge(sig("o_low"), g + 1)
                for n in range(GD):
                    multiply(pl, 8 + GD + n, CR, A_OH + n * CR, 0, CR, oT_hi, oT_lo)

            with pe.Fori(0, GD) as n:
                pl = place_gate(n)
                multiply(pl, 0, CD, 0, 0, CD, hT_hi, hT_lo)
                multiply(pl, 1, CD, CD, 0, CD - 1, hT_hi, hT_lo)
                pe.wait_ge(ada_step, n * KD + (ADA_STEPS + ADA_GATE * KD + KD))
                pe.wait_ge(sig("mods_c"), NG)
                sum_rows(ada_acc[:, 0], XB + 1).then_inc(sig("ada_summed_d"), 1)
                multiply(pl, 1, CD, CD, CD - 1, CD, hT_hi, hT_lo)

            def spread_gain(which):
                pe.wait_ge(sig("gain_diagonal"), which * KD)
                for k in range(KD):
                    last = nc.tensor.matmul(PS[:, XA + k // 4, (k % 4) * P:][:, 0:P], ones,
                                            diagonal(k),
                                            start=True, stop=True)
                last.then_inc(sig("gain_spread"), 1)

            pe.wait_ge(sig("mods_d"), GD)
            spread_gain(1)
            for kp in range(KD // 2):
                if kp < 4:
                    pe.wait_ge(sig("gain_copied"), kp // 2 + 1)
                else:
                    pe.wait_ge(sig("m_low"), kp - 3)
                pe.wait_ge(sig("gated"), kp // 2 + 1)
                transpose_pair(ya, kp, XA + kp % 4).then_inc(sig("m_transposed"), 1)
            with pe.Fori(0, GD // 2) as n:
                pl = place_out(n)
                for j in range(2):
                    for c in range(CD):
                        if j == 0:
                            pe.wait_ge(sig("m_low"), c + 1)
                        multiply(pl, j, CD, j * CD, c, c + 1, hT_hi, hT_lo)

            for kp in range(KD // 2):
                if kp >= 4:
                    pe.wait_ge(sig("h2_scaled"), 2 * (kp - 3))
                for j in range(2):
                    for tt in range(TT):
                        if kp == 0 and j == 0:
                            pe.wait_ge(sig("rms_diagonal"), tt + 1)
                        k = 2 * kp + j
                        last = nc.tensor.matmul(PS[:, XA + kp % 4, (j * TT + tt) * P:][:, 0:P],
                                                yb[:, tt, k * P:(k + 1) * P], by_rms[:, tt], start=True, stop=True)
                last.then_inc(sig("x2_transposed"), 1)

            first = Place(B_FF, G_FF)
            for c in range(CD):
                pe.wait_ge(sig("h2_low"), c + 1)
                multiply(first, 0, CD, 0, c, c + 1, hT_hi, hT_lo)
            multiply(first, 1, CD, CD, 0, CD, hT_hi, hT_lo)

            def hidden_transposed(pl):
                pe.wait_ge(pair_free[pl.pair(-1)], pl.freed(-1) + 1)
                transpose_group(stage, XA).then_inc(sig("ff_transposed"), 1)

            with pe.Fori(1, NF) as n:
                pl = place_ff(n)
                multiply(pl, 0, CD, 0, 0, 4, hT_hi, hT_lo)
                hidden_transposed(pl)
                multiply(pl, 0, CD, 0, 4, CD, hT_hi, hT_lo)
                pe.wait_ge(sig("ff_low"), n)
                for j in range(GD):
                    multiply(pl, 1 + j, CR, CD + j * CR, 0, CR, oT_hi, oT_lo)
                multiply(pl, 1 + GD, CD, CD + GD * CR, 0, CD, hT_hi, hT_lo)
            pl = Place(B_LAST, G_LAST)
            hidden_transposed(pl)
            pe.wait_ge(sig("ff_low"), NF)
            for j in range(GD):
                if j == GD - 1:
                    spread_gain(2)
                multiply(pl, j, CR, j * CR, 0, CR, oT_hi, oT_lo)

        @block.vector
        def _(dve):
            def low(pl, c, width=NW):
                dve.wait_ge(hi_ready, pl.through(c))
                w = KC * width
                s = pl.slot(c)
                nc.vector.tensor_tensor(wlo[:, s, 0:w], raw[:, s, 0:w], whi[:, s, 0:w].bitcast(F32), ALU.subtract)\
                  .then_inc(lo_ready, 1)

            def ada_chunk(group, a, j):
                dve.wait_ge(ada_loaded[a % 2], (group * (CD // 2) + (a // 2 + 1)) * 16)
                for k in range(KC):
                    at = a * KC + k
                    part = ada_raw[:, a % 2, k * NW:(k + 1) * NW]
                    if at == 0:
                        last = nc.vector.tensor_scalar(ada_acc[:, j], part, csilu[:, 0:1], None, ALU.mult)
                    else:
                        dve.wait_ge(ada_step, group * KD + (ADA_STEPS + at))
                        last = nc.vector.scalar_tensor_tensor(
                            out=ada_acc[:, j], in0=part, scalar=csilu[:, at:at + 1], in1=ada_acc[:, j],
                            op0=ALU.mult, op1=ALU.add)
                    last.then_inc(ada_step, 1)

            def piece(group, name):
                at = group * (NW // P)
                nc.vector.tensor_tensor(mods[:, bass.ds(at + 2 * KD, NW // P)], PS[:, XA if name == "b" else XB + 1, 0:NW // P],
                                        vec[:, bass.ds(at + (C_BADA + 2 * KD), NW // P)], ALU.add)\
                  .then_inc(sig("mods_" + name), 1)

            dve.wait_ge(sig("vectors_loaded"), 16)
            dve.wait_ge(sig("c_sigmoid"), 1)
            nc.vector.tensor_tensor(csilu[:], csilu[:], vec[:, C_C:C_C + KD], ALU.mult).then_inc(sig("c_silu"), 1)
            l0, l1 = vec[:, C_LB:C_LB + KD], vec[:, C_LB + KD:C_LB + 2 * KD]
            nc.vector.tensor_tensor(lb[:, 0], l0, l1, ALU.max).then_inc(sig("lb_max"), 1)
            dve.wait_ge(sig("lb_max"), 1)
            nc.vector.tensor_tensor(lb[:, 1], l0, lb[:, 0], ALU.subtract).then_inc(sig("lb_centred"), 1)
            nc.vector.tensor_tensor(lb[:, 2], l1, lb[:, 0], ALU.subtract).then_inc(sig("lb_centred"), 1)
            dve.wait_ge(sig("constants_loaded"), 16)
            dve.wait_ge(sig("positions_loaded"), 16)
            nc.vector.tensor_copy(posf[:], pos[:]).then_inc(sig("pos_float"), 1)
            dve.wait_ge(sig("pos_float"), 1)
            ang, turns = stage[:, 0, 0:TT * HR], stage[:, 0, TT * HR:2 * TT * HR]
            for tt in range(TT):
                nc.vector.tensor_scalar(ang[:, tt * HR:(tt + 1) * HR], con[:, K_FREQ:K_FREQ + HR],
                                        posf[:, tt:tt + 1], None, ALU.mult).then_inc(sig("angle_step"), 1)
            dve.wait_ge(sig("angle_step"), 2)
            nc.vector.tensor_scalar(turns, ang, 1.0 / 6.283185307179586, ROUND, ALU.mult, ALU.add)\
              .then_inc(sig("angle_step"), 1)
            dve.wait_ge(sig("angle_step"), 3)
            nc.vector.tensor_scalar(turns, turns, -ROUND, None, ALU.add).then_inc(sig("angle_step"), 1)
            for i, part in enumerate((TWO_PI_HI, TWO_PI_MID, TWO_PI_LO)):
                dve.wait_ge(sig("angle_step"), 4 + i)
                nc.vector.scalar_tensor_tensor(out=ang, in0=turns, scalar=-part, in1=ang, op0=ALU.mult, op1=ALU.add)\
                  .then_inc(sig("angle_step"), 1)
            dve.wait_ge(sig("angle_step"), 7)
            nc.vector.tensor_scalar(ang, ang, 3.1415925, -3.1415925, ALU.min, ALU.max).then_inc(sig("angle_ready"), 1)
            dve.wait_ge(sig("sin_ready"), 2)
            nc.vector.tensor_tensor(cos[:], cos[:], cos[:], ALU.mult).then_inc(sig("cos_square"), 1)
            dve.wait_ge(sig("cos_square"), 1)
            nc.vector.tensor_scalar(cos[:], cos[:], -2.0, 1.0, ALU.mult, ALU.add).then_inc(sig("cos_ready"), 1)
            dve.wait_ge(sig("lb_exp"), 1)
            nc.vector.tensor_tensor(lb[:, 3], lb[:, 1], lb[:, 2], ALU.add).then_inc(sig("lb_step"), 1)
            dve.wait_ge(sig("lb_step"), 1)
            nc.vector.reciprocal(lb[:, 3], lb[:, 3]).then_inc(sig("lb_step"), 1)
            dve.wait_ge(sig("lb_step"), 2)
            nc.vector.tensor_tensor(lb[:, 1], lb[:, 1], lb[:, 3], ALU.mult).then_inc(sig("lb_step"), 1)
            dve.wait_ge(sig("lb_step"), 3)
            nc.vector.tensor_scalar(lb[:, 2], lb[:, 1], -1.0, 1.0, ALU.mult, ALU.add).then_inc(sig("lb_step"), 1)

            def rsqrt_of(src, n, name, count=0, between=None):
                nc.vector.tensor_scalar(src, src, 1.0 / n, EPS, ALU.mult, ALU.add).then_inc(sig(name + "_mean"), 1)
                if between:
                    between()
                dve.wait_ge(sig(name + "_rsqrt"), count + 1)

            dve.wait_ge(sig("x_squared"), TT)
            rsqrt_of(stat[:, 0:TT], D, "trunk")
            for tt in range(TT):
                nc.vector.tensor_scalar(ya[:, tt], ya[:, tt], stat[:, tt:tt + 1], None, ALU.mult)\
                  .then_inc(sig("x_scaled"), 1)

            dve.wait_ge(sig("c_silu"), 1)

            def first_groups(i):
                for j in range(2):
                    if not isinstance(i, int):
                        dve.wait_ge(sig(f"ada0_summed{j}"), i)
                    for at in range(KD):
                        c, k = j * CD + at // KC, at % KC
                        part = raw[:, c % RING, k * NW:(k + 1) * NW]
                        if k == 0:
                            dve.wait_ge(raw_loaded[c % RING], (i * (2 * CD // RING) + (c // RING + 1)) * 16)
                        if at == 0:
                            last = nc.vector.tensor_scalar(ada_acc[:, j], part, csilu[:, 0:1], None, ALU.mult)
                        else:
                            dve.wait_ge(ada_step, i * (2 * KD) + (j * KD + at))
                            last = nc.vector.scalar_tensor_tensor(
                                out=ada_acc[:, j], in0=part, scalar=csilu[:, at:at + 1], in1=ada_acc[:, j],
                                op0=ALU.mult, op1=ALU.add)
                        last.then_inc(ada_step, 1)

            first_groups(0)
            with dve.Fori(1, GD) as i:
                first_groups(i)
            for j in range(2):
                dve.wait_ge(sig(f"ada0_summed{j}"), GD)
            nc.vector.tensor_tensor(mods[:, 0:2 * KD], PS[:, XA, 0:2 * KD], vec[:, C_BADA:C_BADA + 2 * KD], ALU.add)\
              .then_inc(sig("mods0"), 1)
            dve.wait_ge(sig("mods0"), 1)
            nc.vector.scalar_tensor_tensor(out=scale_h[:], in0=mods[:, SC_M:SC_M + KD], scalar=1.0,
                                           in1=vec[:, C_GPRE:C_GPRE + KD], op0=ALU.add, op1=ALU.mult)\
              .then_inc(sig("scale_h_ready"), 1)
            dve.wait_ge(sig("scale_h_ready"), 1)
            for kp in range(KD // 2):
                dve.wait_ge(sig("xT_copied"), kp + 1)
                for j in range(2):
                    k = 2 * kp + j
                    seg = xT[:, kp, j * T:(j + 1) * T]
                    last = nc.vector.tensor_scalar(seg, seg, scale_h[:, k:k + 1], mods[:, SH_M + k:SH_M + k + 1],
                                                   ALU.mult, ALU.add)
                last.then_inc(sig("h_scaled"), 1)
                if kp:
                    dve.wait_ge(sig("h_high"), kp)
                    nc.vector.tensor_tensor(pairs(hT_lo, kp - 1), xT[:, kp - 1], pairs(hT_hi, kp - 1).bitcast(F32),
                                            ALU.subtract).then_inc(sig("h_low"), 1)
            dve.wait_ge(sig("h_high"), KD // 2)
            nc.vector.tensor_tensor(pairs(hT_lo, KD // 2 - 1), xT[:, KD // 2 - 1],
                                    pairs(hT_hi, KD // 2 - 1).bitcast(F32), ALU.subtract).then_inc(sig("h_low"), 1)

            pl = place_c()

            def lows(a, b):
                for c in range(a, b):
                    low(pl, c, ROPE if 2 * CD <= c < 3 * CD else NW)

            def normed(j, src):
                dve.wait_ge(sig("c_squared"), 2 * (j + 1))
                rsqrt_of(stat[:, 4 + 2 * j:6 + 2 * j], LORA, "c", j)
                for tt in range(TT):
                    nc.vector.tensor_scalar(src[:, tt], src[:, tt], stat[:, 4 + 2 * j + tt:5 + 2 * j + tt], None,
                                            ALU.mult).then_inc(sig("c_normed"), 1)

            def gained(j):
                dve.wait_ge(sig("c_transposed"), j + 1)
                for k in range(LORA // P):
                    gain = vec[:, C_GQ + j * (LORA // P) + k:][:, 0:1]
                    nc.vector.tensor_scalar(zT[:, j, k * T:(k + 1) * T], by_ktile(XA)[:, k], gain, None, ALU.mult)\
                      .then_inc(sig("c_scaled"), 1)
                dve.wait_ge(sig("c_high"), j + 1)
                nc.vector.tensor_tensor(cT_lo[:, j].rearrange("p k t -> p (k t)"), zT[:, j],
                                        cT_hi[:, j].rearrange("p k t -> p (k t)").bitcast(F32),
                                        ALU.subtract).then_inc(sig("c_low"), 1)

            def rotate(src, dst, parts, heads, free, done, count):
                a, b = src[:, :, :, 0:HR], src[:, :, :, HR:ROPE]
                co = cos[:].unsqueeze(2).broadcast_to([P, TT, heads, HR])
                si = sin[:].unsqueeze(2).broadcast_to([P, TT, heads, HR])
                n = TT * heads * HR
                pr = [parts[:, i * n:(i + 1) * n].rearrange("p (t h d) -> p t h d", t=TT, h=heads) for i in range(4)]
                nc.vector.tensor_tensor(pr[0], a, co, ALU.mult)
                nc.vector.tensor_tensor(pr[1], b, si, ALU.mult)
                nc.vector.tensor_tensor(pr[2], b, co, ALU.mult)
                nc.vector.tensor_tensor(pr[3], a, si, ALU.mult).then_inc(free[0], 1)
                dve.wait_ge(free[0], free[1] + 1)
                nc.vector.tensor_tensor(dst[:, :, :, 0:HR], pr[0], pr[1], ALU.subtract)
                nc.vector.tensor_tensor(dst[:, :, :, HR:ROPE], pr[2], pr[3], ALU.add).then_inc(sig(done), 1)

            def add_pair(pl, g, c, dst):
                dve.wait_ge(multiplied, pl.through(c))
                p = pl.pair(g)
                nc.vector.tensor_tensor(dst, dst, banks(2 * p), ALU.add).then_inc(pair_free[p], 1)

            lows(0, CD + 3)
            normed(0, stage)
            lows(CD + 3, 2 * CD + 3)
            gained(0)
            normed(1, side)
            lows(2 * CD + 3, 3 * CD + AHEAD)
            gained(1)
            dve.wait_ge(multiplied, pl.through(3 * CD - 1))
            dve.wait_ge(sig("cos_ready"), 1)
            rotate(PS[:, 0:2, 0:ROPE].unsqueeze(2), qT[:, 0:TT, 0:ROPE].unsqueeze(2), flat(kT), 1,
                   (pair_free[0], 1), "kr_rotated", 0)

            dve.wait_ge(sig("sums_zeroed"), 2)
            with dve.Fori(0, NG) as g:
                pl = place_a(g)

                def steps(a, b):
                    for c in range(a, b):
                        low(pl, c, NW // 2 if A_UR <= c < A_UV else NW)
                        i = c - A_ADA
                        if 0 <= i < ADA_A * CD:
                            j = i // CD
                            if i == 2 * CD:
                                dve.wait_ge(sig("ada_summed_a"), g + 1)
                            ada_chunk(g * ADA_A + j, i % CD, j % 2)

                steps(AHEAD, 8)
                dve.wait_ge(multiplied, pl.through(A_UV - 1))
                p = pl.pair(2)
                rotate(PS[:, 2 * p:2 * p + 2, 0:NW // 2].rearrange("p t (h d) -> p t h d", h=HPG), rotated,
                       zT[:, 0], HPG, (pair_free[p], pl.freed(2)), "qr_rotated", g)
                steps(8, 15)
                dve.wait_ge(sig("scored"), g + 1)
                nc.vector.tensor_tensor(prob[:, :, 0:3:2, :], by_tile(XA).rearrange("p (h two) s -> p h two s", two=2),
                                        con[:, K_NEG:K_NEG + P].unsqueeze(1).unsqueeze(1).broadcast_to([P, HPG, 2, P]),
                                        ALU.add).then_inc(sig("scores_masked"), 1)
                dve.wait_ge(sig("scores_masked"), g + 1)
                nc.vector.tensor_reduce(stat[:, 16:16 + HPG], prob[:, :, 0, :], AX.X, ALU.max)
                dve.wait_ge(sig("scores_copied"), g + 1)
                nc.vector.tensor_reduce(stat[:, 16 + HPG:16 + 2 * HPG], prob[:, :, 1:3, :], AX.XY, ALU.max)\
                  .then_inc(sig("max_found"), 1)
                dve.wait_ge(sig("max_found"), g + 1)
                nc.vector.tensor_scalar(stat[:, 16:24], stat[:, 16:24], -SCALE, None, ALU.mult)\
                  .then_inc(sig("max_ready"), 1)
                dve.wait_ge(sig("ada_summed_a"), g + 1)
                piece(g * ADA_A, "a")
                steps(15, 21)
                dve.wait_ge(sig("exps"), g * 8 + 8)
                nc.vector.reciprocal(stat[:, 24:32], stat[:, 24:32]).then_inc(sig("sums_inverted"), 1)
                steps(21, 23)
                dve.wait_ge(sig("ada_summed_b"), g + 1)
                piece(g * ADA_A + 1, "b")
                dve.wait_ge(sig("att_summed"), g + 1)
                dve.wait_ge(sig("sums_inverted"), g + 1)
                nc.vector.tensor_tensor(side[:].rearrange("p t (h c) -> p (t h) c", c=P), by_tile(XB),
                                        stat[:, 24:32].unsqueeze(2).broadcast_to([P, 2 * HPG, P]), ALU.mult)\
                  .then_inc(sig("att_scaled"), 1)
                steps(23, 25)
                dve.wait_ge(sig("att_high"), g + 1)
                nc.vector.tensor_tensor(attT_lo[:], by_ktile(XA), attT_hi[:].bitcast(F32), ALU.subtract)\
                  .then_inc(sig("att_low"), 1)
                steps(25, 27)
                dve.wait_ge(sig("f_sigmoid"), g + 1)
                for h in range(HPG):
                    f = kT[:, TT * h:TT * (h + 1), :].rearrange("p i s -> p (i s)")
                    nc.vector.tensor_scalar(f, f, lb[:, 2, bass.ds(g * HPG + h, 1)], lb[:, 1, bass.ds(g * HPG + h, 1)],
                                            ALU.mult, ALU.add).then_inc(sig("f_ready"), 1)
                steps(27, 30)
                dve.wait_ge(sig("q_sigmoid"), g + 1)
                nc.vector.tensor_tensor(qT[:], qT[:], by_tile(XA), ALU.mult).then_inc(sig("q_ready"), 1)
                dve.wait_ge(sig("log_f"), g + 1)
                nc.vector.tensor_scalar(flat(kT), flat(kT), -1.0, 1.0, ALU.mult, ALU.add).then_inc(sig("k_ready"), 1)
                for i in range(2 * HPG):
                    nc.vector.tensor_tensor_scan(bT[:, i], ones, bT[:, i], 0.0, ALU.mult, ALU.add)\
                      .then_inc(sig("b_ready"), 1)
                steps(30, 31)

                def differences(L):
                    d = dec[:, L % 2]
                    if L >= 2:
                        dve.wait_ge(sig("decayed"), g * 8 + (L - 1))
                    if L == len(LEVELS):
                        b = tiles(flat(bT))
                        end = b[:, :, 0, P - 1:P].broadcast_to([P, HPG, P])
                        last = nc.vector.tensor_tensor(tiles(d)[:, :, 0, :], end, b[:, :, 0, :], ALU.subtract)
                    else:
                        m = LEVELS[L]
                        b, d = halves(flat(bT), m), halves(d, m)
                        end = b[:, :, 0, m - 1:m].broadcast_to([P, HPG * P // m, m])
                        nc.vector.tensor_tensor(d[:, :, 1, :], b[:, :, 1, :], end, ALU.subtract)
                        last = nc.vector.tensor_tensor(d[:, :, 0, :], end, b[:, :, 0, :], ALU.subtract)
                    last.then_inc(sig("diffs"), 1)

                def decay(L):
                    view = tiles if L == len(LEVELS) else lambda f: halves(f, LEVELS[L])
                    d, z = view(dec[:, L % 2]), view(zT[:, L % 2])
                    n = len(LEVELS) + 2
                    dve.wait_ge(sig("decays"), g * n + (L + 1 + (L == len(LEVELS))))
                    if L >= 2:
                        dve.wait_ge(sig(f"level{L - 2}_scored"), g + 1)
                    nc.vector.tensor_tensor(z[:, :, 1, :], view(flat(qT))[:, :, 1, :], d[:, :, 1, :], ALU.mult)
                    nc.vector.tensor_tensor(z[:, :, 0, :], view(flat(kT))[:, :, 0, :], d[:, :, 0, :], ALU.mult)\
                      .then_inc(sig("decayed"), 1)

                def merge(L):
                    m = LEVELS[L]
                    dve.wait_ge(sig("masks_loaded"), 16)
                    dve.wait_ge(sig(f"level{L}_scored"), g + 1)
                    dve.wait_ge(sig(f"level{L - 1}_merged" if L else "self_merged"), g + 1)
                    shape = [P, 2 * HPG, P // (2 * m), m]
                    o = pT[:].rearrange("p i (x two m) -> p i x two m", two=2, m=m)[:, :, :, 1, :]
                    mask = msk[:, L * 64:(L + 1) * 64].rearrange("p (x m) -> p x m", m=m)
                    nc.vector.copy_predicated(o, mask.unsqueeze(1).broadcast_to(shape),
                                              PS[:, XA + L % 4, :].rearrange("p (i x m) -> p i x m", i=2 * HPG, m=m))\
                      .then_inc(sig(f"level{L}_merged"), 1)

                dve.wait_ge(sig("b_ready"), g * 8 + 8)
                differences(0)
                for L in range(len(LEVELS) + 1):
                    steps(31 + 2 * L, 32 + 2 * L)
                    if L < len(LEVELS):
                        differences(L + 1)
                    if L:
                        merge(L - 1)
                    steps(32 + 2 * L, 33 + 2 * L)
                    decay(L)
                    if L == 0:
                        dve.wait_ge(sig("masks_loaded"), 16)
                        dve.wait_ge(sig("self_scored"), g + 1)
                        nc.vector.copy_predicated(pT[:], msk[:, len(LEVELS) * 64:].unsqueeze(1)
                                                  .broadcast_to([P, 2 * HPG, P]), by_tile(XB))\
                          .then_inc(sig("self_merged"), 1)
                    if 32 + 2 * L == 44:
                        dve.wait_ge(sig("og_sigmoid"), g + 1)
                        p = pl.pair(7)
                        nc.vector.tensor_tensor(side[:], side[:], banks(2 * p), ALU.mult).then_inc(pair_free[p], 1)
                        dve.wait_ge(pair_free[p], pl.freed(7) + 1)
                        s3 = side[:].rearrange("p t (h c) -> p (t h) c", c=P)
                        nc.vector.tensor_tensor(s3, s3, con[:, K_GHG:K_GHG + P].unsqueeze(1)
                                                .broadcast_to([P, 2 * HPG, P]), ALU.mult).then_inc(sig("og_ready"), 1)
                    if 32 + 2 * L in (44, 46):
                        n = (32 + 2 * L - 44) // 2
                        add_pair(pl, 8 + n, A_OM + 2 * n + 1, yb[:, :, n * NW:(n + 1) * NW])
                steps(47, 49)
                dve.wait_ge(sig("o_squared"), g + 1)
                nc.vector.tensor_reduce(stat[:, 32:40], dec[:, 0].rearrange("p (i s) -> p i s", s=P), AX.X, ALU.add)\
                  .then_inc(sig("o_square_sum"), 1)
                dve.wait_ge(sig("o_square_sum"), g + 1)
                rsqrt_of(stat[:, 32:40], P, "o", g)
                nc.vector.tensor_tensor(dec[:, 1].rearrange("p (i s) -> p i s", s=P), by_tile(XB),
                                        stat[:, 32:40].unsqueeze(2).broadcast_to([P, 2 * HPG, P]), ALU.mult)\
                  .then_inc(sig("o_normed"), 1)
                dve.wait_ge(sig("o_normed"), g + 1)
                dve.wait_ge(sig("og_ready"), g + 1)
                nc.vector.tensor_tensor(stage[:], gates(1), side[:], ALU.mult).then_inc(sig("o_gated"), 1)
                add_pair(pl, 10, A_OM + 5, yb[:, :, 2 * NW:3 * NW])
                steps(49, 51)
                add_pair(pl, 11, A_OM + 7, yb[:, :, 3 * NW:4 * NW])
                dve.wait_ge(sig("o_high"), g + 1)
                nc.vector.tensor_tensor(oT_lo[:], by_ktile(XA), oT_hi[:].bitcast(F32), ALU.subtract)\
                  .then_inc(sig("o_low"), 1)
                steps(51, 53)
                add_pair(pl, 12, A_OH + 1, ya[:, :, 0:NW])
                dve.wait_ge(sig("ada_summed_c"), g + 1)
                piece(g * ADA_A + 2, "c")
                steps(53, 55)
                add_pair(pl, 13, A_OH + 3, ya[:, :, NW:2 * NW])
                steps(55, 57)
                add_pair(pl, 14, A_OH + 5, ya[:, :, 2 * NW:3 * NW])
                steps(57, A_N + AHEAD)
                add_pair(pl, 15, A_OH + 7, ya[:, :, 3 * NW:4 * NW])

            def make_gain(which, c_gain, piece_at):
                nc.vector.tensor_tensor(gain_y[:], vec[:, c_gain:c_gain + KD], mods[:, piece_at:piece_at + KD],
                                        ALU.mult).then_inc(sig("gain_ready"), 1)
                dve.wait_ge(sig("gain_ready"), which)
                for k in range(KD):
                    nc.vector.tensor_scalar(diagonal(k), ident, gain_y[:, k:k + 1], None, ALU.mult)\
                      .then_inc(sig("gain_diagonal"), 1)

            dve.wait_ge(sig("mods_c"), NG)
            make_gain(1, C_GPOST, GA_M)
            with dve.Fori(0, GD) as n:
                pl = place_gate(n)
                cols = bass.ds(n * NW, NW)
                for c in range(AHEAD, 2 * CD + AHEAD):
                    low(pl, c)
                    i = c - G_ADA
                    if i == 0:
                        dve.wait_ge(sig("ada_summed_c"), NG)
                    if 0 <= i < CD:
                        ada_chunk(n + ADA_GATE, i, 0)
                    if c == CD + 3:
                        dve.wait_ge(pair_free[pl.pair(0)], pl.freed(0) + 1)
                        nc.vector.tensor_tensor(gates(0), gates(0), ya[:, :, cols], ALU.mult)\
                          .then_inc(sig("gated_a"), 1)
                dve.wait_ge(sig("ada_summed_d"), n + 1)
                piece(n + ADA_GATE, "d")
                dve.wait_ge(pair_free[pl.pair(1)], pl.freed(1) + 1)
                nc.vector.tensor_tensor(gates(1), gates(1), yb[:, :, cols], ALU.mult).then_inc(sig("gated_b"), 1)
                dve.wait_ge(sig("gated_a"), n + 1)
                dve.wait_ge(sig("gated_b"), n + 1)
                nc.vector.tensor_tensor(ya[:, :, cols], gates(0), gates(1), ALU.add).then_inc(sig("gated"), 1)

            for kp in range(KD // 2):
                dve.wait_ge(sig("m_high"), kp + 1)
                nc.vector.tensor_tensor(pairs(hT_lo, kp), PS[:, XA + kp % 4, :], pairs(hT_hi, kp).bitcast(F32),
                                        ALU.subtract).then_inc(sig("m_low"), 1)

            dve.wait_ge(sig("mods_d"), GD)
            nc.vector.scalar_tensor_tensor(out=scale_h[:], in0=mods[:, SC_F:SC_F + KD], scalar=1.0,
                                           in1=vec[:, C_GPRE2:C_GPRE2 + KD], op0=ALU.add, op1=ALU.mult)\
              .then_inc(sig("scale_h_ready"), 1)
            with dve.Fori(0, GD // 2) as n:
                pl = place_out(n)
                for j in range(2):
                    for c in range(j * CD + AHEAD, (j + 1) * CD + AHEAD):
                        low(pl, c)
                    dve.wait_ge(multiplied, pl.through((j + 1) * CD - 1))
                    p = pl.pair(j)
                    dve.wait_ge(sig("y_squared"), n * (2 * TT) + (j + 1) * TT)
                    nc.vector.tensor_tensor(ya[:, :, bass.ds(n * (2 * NW) + j * NW, NW)], banks(2 * p),
                                            gain_row[:, bass.ds(n * (2 * NW) + j * NW, NW)].unsqueeze(1)
                                            .broadcast_to([P, TT, NW]), ALU.mult)\
                      .then_inc(pair_free[p], 1)

            def reciprocal_rms(at, count, between=None):
                nc.vector.tensor_reduce(stat[:, at:at + TT], sums[:], AX.X, ALU.add)\
                  .then_inc(sig("squares_summed"), 1)
                dve.wait_ge(sig("squares_summed"), 1 if count == 1 else 2)
                rsqrt_of(stat[:, at:at + TT], D, "trunk", count, between)

            reciprocal_rms(8, 1)
            dve.wait_ge(sig("x_again"), 16)
            dve.wait_ge(pair_free[0], freed_by(0, G_FF))
            dve.wait_ge(pair_free[1], freed_by(1, G_FF))
            for tt in range(TT):
                nc.vector.scalar_tensor_tensor(out=yb[:, tt], in0=ya[:, tt], scalar=stat[:, 8 + tt:9 + tt],
                                               in1=yb[:, tt], op0=ALU.mult, op1=ALU.add)\
                  .then_inc(sig("x_mixed"), 1)
            dve.wait_ge(sig("x2_squared"), TT)
            rsqrt_of(stat[:, 10:10 + TT], D, "trunk", 2)
            for tt in range(TT):
                nc.vector.tensor_scalar(by_rms[:, tt], ident, stat[:, 10 + tt:11 + tt], None, ALU.mult)\
                  .then_inc(sig("rms_diagonal"), 1)
            dve.wait_ge(sig("scale_h_ready"), 2)

            def h2_low(kp):
                dve.wait_ge(sig("h2_high"), kp + 1)
                nc.vector.tensor_tensor(pairs(hT_lo, kp), dec[:, kp % 2, 0:NW], pairs(hT_hi, kp).bitcast(F32),
                                        ALU.subtract).then_inc(sig("h2_low"), 1)

            for kp in range(KD // 2):
                dve.wait_ge(sig("x2_transposed"), kp + 1)
                if kp >= 2:
                    dve.wait_ge(sig("h2_low"), kp - 1)
                for j in range(2):
                    k = 2 * kp + j
                    nc.vector.tensor_scalar(dec[:, kp % 2, j * T:(j + 1) * T], PS[:, XA + kp % 4, j * T:(j + 1) * T],
                                            scale_h[:, k:k + 1], mods[:, SH_F + k:SH_F + k + 1], ALU.mult, ALU.add)\
                      .then_inc(sig("h2_scaled"), 1)
                if kp:
                    h2_low(kp - 1)
            h2_low(KD // 2 - 1)
            nc.vector.memset(ya[:], 0.0)
            make_gain(2, C_GPOST2, GA_F)

            def hidden(pl):
                dve.wait_ge(multiplied, pl.through(-1))
                p = pl.pair(-1)
                nc.vector.tensor_tensor(stage[:], stage[:], banks(2 * p), ALU.mult).then_inc(pair_free[p], 1)

            def hidden_low(n):
                dve.wait_ge(sig("ff_high"), n)
                nc.vector.tensor_tensor(oT_lo[:], by_ktile(XA), oT_hi[:].bitcast(F32), ALU.subtract)\
                  .then_inc(sig("ff_low"), 1)

            def silu_gate(pl, n):
                dve.wait_ge(sig("ff_sigmoid"), n)
                p = pl.pair(0)
                nc.vector.tensor_tensor(stage[:], stage[:], banks(2 * p), ALU.mult).then_inc(pair_free[p], 1)

            first = Place(B_FF, G_FF)
            for c in range(AHEAD, 2 * CD):
                low(first, c)
                if c == CD + 3:
                    silu_gate(first, 1)
            with dve.Fori(1, NF) as n:
                pl = place_ff(n)
                for c in range(F_N):
                    low(pl, c)
                    if c == 3:
                        hidden(pl)
                    if c == 6:
                        hidden_low(n)
                    if c == CD + 3:
                        silu_gate(pl, n + 1)
                    j = c - CD - CR - 2
                    if j in (0, 2, 4, 6):
                        j //= 2
                        add_pair(pl, 1 + j, CD + j * CR + CR - 1, ya[:, :, j * NW:(j + 1) * NW])
            pl = Place(B_LAST, G_LAST)

            def add_out(j):
                dve.wait_ge(multiplied, pl.through(j * CR + CR - 1))
                cols = slice(j * NW, (j + 1) * NW)
                p = pl.pair(j)
                nc.vector.tensor_tensor(ya[:, :, cols], ya[:, :, cols], banks(2 * p), ALU.add)\
                  .then_inc(pair_free[p], 1)
                dve.wait_ge(pair_free[p], pl.freed(j) + 1)

            def gain_out(j):
                cols = slice(j * NW, (j + 1) * NW)
                dve.wait_ge(sig("y2_squared"), (j + 1) * TT)
                nc.vector.tensor_tensor(ya[:, :, cols], ya[:, :, cols], PS[:, XA + j, :].unsqueeze(1)
                                        .broadcast_to([P, TT, NW]), ALU.mult).then_inc(sig("y2_gained"), 1)

            for c in range(GD * CR):
                low(pl, c)
                if c == 3:
                    hidden(pl)
                    hidden_low(NF)
                if c in (4, 6):
                    add_out((c - 4) // 2)
            dve.wait_ge(sig("gain_spread"), 2)
            gain_out(0)
            for j in range(2, GD):
                add_out(j)
                gain_out(j - 1)
            dve.wait_ge(sig("y2_squared"), GD * TT)
            reciprocal_rms(12, 3, lambda: gain_out(GD - 1))
            for n in range(GD):
                cols = slice(n * NW, (n + 1) * NW)
                dve.wait_ge(sig("y2_gained"), n + 1)
                for tt in range(TT):
                    nc.vector.scalar_tensor_tensor(out=yb[:, tt, cols], in0=ya[:, tt, cols],
                                                   scalar=stat[:, 12 + tt:13 + tt], in1=yb[:, tt, cols],
                                                   op0=ALU.mult, op1=ALU.add).then_inc(sig("x_final"), 1)


def _by_columns(w, width=NW):
    k, n = w.shape
    return w.reshape(k // (KC * P), KC, P, n // width, width).transpose(3, 0, 2, 1, 4)\
            .reshape(n // width, k // (KC * P), P, KC * width)


def _by_rows(w):
    k, n = w.shape
    return w.reshape(k // NW, CR, KC, P, n // NW, NW).transpose(0, 4, 1, 3, 2, 5)\
            .reshape(k // NW, n // NW, CR, P, KC * NW)


def _columns(a):
    return a.reshape(-1, P).T


def kernel(x, c, positions, w_ada, b_ada, g_pre_mix, w_in, lb_logits, g_hg_out, w_o_hg, g_q_lora, w_uq,
           g_kv_lora, w_ukv, w_o_mla, w_out, g_post_mix, g_pre_ffn, w_gate_up, w_down, g_post_ffn):
    import concourse.bacc as bacc
    import numpy as np
    from concourse.bass_utils import run_bass_kernel_spmd

    f32 = np.float32
    (x, c, positions, w_ada, b_ada, g_pre_mix, w_in, lb_logits, g_hg_out, w_o_hg, g_q_lora, w_uq, g_kv_lora,
     w_ukv, w_o_mla, w_out, g_post_mix, g_pre_ffn, w_gate_up, w_down, g_post_ffn) = (
        np.asarray(a) for a in (x, c, positions, w_ada, b_ada, g_pre_mix, w_in, lb_logits, g_hg_out, w_o_hg,
                                g_q_lora, w_uq, g_kv_lora, w_ukv, w_o_mla, w_out, g_post_mix, g_pre_ffn,
                                w_gate_up, w_down, g_post_ffn))
    vectors = np.concatenate([_columns(a) for a in (c[0], b_ada[0], g_pre_mix[0], g_post_mix[0], g_pre_ffn[0],
                                                    g_post_ffn[0], g_q_lora[0], g_kv_lora[0], lb_logits[0],
                                                    lb_logits[1])], axis=1)
    i = np.arange(P)
    freq = (np.float32(10000.0) ** (-np.arange(0, ROPE, 2, dtype=f32) / f32(ROPE))).astype(f32)
    consts = np.concatenate([np.eye(P, dtype=f32), np.where(i[None, :] <= i[:, None], 0, -1e30).astype(f32),
                             np.ones((P, P), f32), np.broadcast_to(g_hg_out[0], (P, P)),
                             np.broadcast_to(freq, (P, HR)), np.full((P, TT * HPG), -0.5, f32)], axis=1)
    masks = np.zeros((P, len(LEVELS) * 64 + P), np.int32)
    for L, m in enumerate(LEVELS):
        j = np.arange(64)
        t = j // m * 2 * m + m + j % m
        masks[:, L * 64:(L + 1) * 64] = (i[:, None] // (2 * m) == t[None, :] // (2 * m)) & (i[:, None] % (2 * m) < m)
    masks[:, len(LEVELS) * 64:] = np.eye(P, dtype=np.int32)

    w_in, w_ada, w_uq, w_ukv, w_gate_up = w_in[0], w_ada[0], w_uq[0], w_ukv[0], w_gate_up[0]
    heads = D // P
    uq = w_uq.reshape(LORA, heads, P + ROPE)
    ukv = w_ukv.reshape(LORA, heads, 2 * P)
    ada = _by_columns(w_ada)
    at = 4 * D
    host = {
        "x": x[0].reshape(TT, P, D).transpose(1, 0, 2),
        "vectors": vectors, "consts": consts, "masks": masks, "positions": positions[0].reshape(TT, P).T,
        "ada0": ada[:2 * GD].reshape(-1, P, KC * NW), "ada1": ada[2 * GD:].reshape(-1, P, KC * NW),
        "w_c": _by_columns(w_in[:, at:at + 2 * LORA]).reshape(-1, P, KC * NW),
        "w_kr": _by_columns(w_in[:, at + 2 * LORA:at + 2 * LORA + ROPE], ROPE)[0],
        "w_uqn": _by_columns(uq[:, :, :P].reshape(LORA, -1)),
        "w_uqr": _by_columns(uq[:, :, P:].reshape(LORA, -1), NW // 2),
        "w_uk": _by_columns(ukv[:, :, :P].reshape(LORA, -1)),
        "w_uv": _by_columns(ukv[:, :, P:].reshape(LORA, -1)),
        "w_hf": _by_columns(w_in[:, D:2 * D]), "w_hq": _by_columns(w_in[:, :D]),
        "w_hi": _by_columns(w_in[:, 2 * D:3 * D]), "w_hg": _by_columns(w_in[:, 3 * D:4 * D]),
        "w_omla": _by_rows(w_o_mla[0]), "w_ohg": _by_rows(w_o_hg[0]),
        "w_ga": _by_columns(w_in[:, -2 * D:-D]), "w_gb": _by_columns(w_in[:, -D:]),
        "w_out": _by_columns(w_out[0]),
        "w_gate": _by_columns(w_gate_up[:, :D_FF]), "w_up": _by_columns(w_gate_up[:, D_FF:]),
        "w_down": _by_rows(w_down[0]),
    }
    nc = bacc.Bacc("TRN2", target_bir_lowering=False, num_devices=1, dynamic_dma_scratch_size=1024)
    arrays, args = {}, []
    for name, a in host.items():
        a = np.ascontiguousarray(a)
        arrays["in_" + name] = a
        args.append(nc.dram_tensor("in_" + name, a.shape, mybir.dt.from_np(a.dtype), kind="ExternalInput").ap())
    args.append(nc.dram_tensor("out", (P, TT, D), F32, kind="ExternalOutput").ap())
    build(nc, *args)
    y = run_bass_kernel_spmd(nc, [arrays], core_ids=[0]).results[0]["out"]
    return y.reshape(P, TT, D).transpose(1, 0, 2).reshape(1, T, D)
```

```python
from contextlib import ExitStack

import concourse.bass as bass
from concourse import mybir

F32 = mybir.dt.float32
F32R = mybir.dt.float32r
I32 = mybir.dt.int32

ACT = mybir.ActivationFunctionType
ALU = mybir.AluOpType
AX = mybir.AxisListType

P = 128
TT = 2
T = TT * P
D = 2048
KD = D // P
NW = 512
KC = 2
GD = D // NW
CD = KD // KC
HPG = NW // P
NG = D // NW
ROPE = 64
HR = ROPE // 2
LORA = 512
CL = LORA // P // KC
CR = NW // P // KC
D_FF = 5632
NF = D_FF // NW
N_MOD = 6
EPS = 1e-6
SCALE = float(P + ROPE) ** -0.5
RING = 4
AHEAD = RING - 1
LEVELS = [64, 32, 16, 8, 4, 2, 1]
ADA_A = 3
TWO_PI_HI, TWO_PI_MID = 6.28125, 0.00193500518798828125
TWO_PI_LO = 6.283185307179586 - TWO_PI_HI - TWO_PI_MID
ROUND = 12582912.0

C_C, C_BADA = 0, KD
C_GPRE, C_GPOST, C_GPRE2, C_GPOST2 = (C_BADA + N_MOD * KD + KD * i for i in range(4))
C_GQ = C_GPOST2 + KD
C_GKV = C_GQ + LORA // P
C_LB = C_GKV + LORA // P
C_END = C_LB + 2 * KD
K_ID, K_NEG, K_ONE, K_GHG, K_FREQ = 0, P, 2 * P, 3 * P, 4 * P
K_POW = K_FREQ + HR
K_END = K_POW + TT * HPG
SH_M, SC_M, GA_M, SH_F, SC_F, GA_F = (i * KD for i in range(N_MOD))


class Place:

    def __init__(self, chunk, group, chunks=0, groups=0, i=0):
        self.chunk, self.group, self.chunks, self.groups, self.i = chunk, group, chunks, groups, i

    def slot(self, c):
        return (self.chunk + c) % RING

    def turn(self, c):
        return (self.chunk + c) // RING + self.i * (self.chunks // RING)

    def through(self, c):
        return self.i * self.chunks + (self.chunk + c + 1)

    def pair(self, g):
        return (self.group + g) % 2

    def starts(self, c):
        return self.chunks == 0 and self.chunk + c < RING

    def fresh(self, g):
        return self.groups == 0 and self.group + g < 2

    def freed(self, g):
        return self.i * (self.groups // 2) + (self.group + g) // 2


def build(nc, x, vectors, consts, masks, positions, ada0, ada1, w_c, w_kr, w_uqn, w_uqr, w_uk, w_uv, w_hf,
          w_hq, w_hi, w_hg, w_omla, w_ohg, w_ga, w_gb, w_out, w_gate, w_up, w_down, out):
    ctx = ExitStack()
    with ctx:
        def sb(name, shape, dt=F32):
            return ctx.enter_context(nc.sbuf_tensor(name, shape, dt))

        raw = sb("raw", [P, RING, KC * NW])
        whi = sb("whi", [P, RING, KC * NW], F32R)
        wlo = sb("wlo", [P, RING, KC * NW], F32R)
        ada_raw = sb("ada_raw", [P, 2, KC * NW])
        ada_acc = sb("ada_acc", [P, 2, NW])
        hT_hi = sb("hT_hi", [P, KD, T], F32R)
        hT_lo = sb("hT_lo", [P, KD, T], F32R)
        cT_hi = sb("cT_hi", [P, 2, LORA // P, T], F32R)
        cT_lo = sb("cT_lo", [P, 2, LORA // P, T], F32R)
        ya = sb("ya", [P, TT, D])
        yb = sb("yb", [P, TT, D])
        stage = sb("stage", [P, TT, NW])
        side = sb("side", [P, TT, NW])
        qT = sb("qT", [P, 2 * HPG, P])
        kT = sb("kT", [P, 2 * HPG, P])
        bT = sb("bT", [P, 2 * HPG, P])
        dec = sb("dec", [P, 2, 2 * HPG * P])
        zT = sb("zT", [P, 2, 2 * HPG * P])
        pT = sb("pT", [P, 2 * HPG, P])
        pTx = sb("pTx", [P, HPG, P])
        v = sb("v", [P, TT, NW])
        attT_hi = sb("attT_hi", [P, HPG, T], F32R)
        attT_lo = sb("attT_lo", [P, HPG, T], F32R)
        oT_hi = sb("oT_hi", [P, HPG, T], F32R)
        oT_lo = sb("oT_lo", [P, HPG, T], F32R)
        vec = sb("vec", [P, C_END])
        con = sb("con", [P, K_END])
        msk = sb("msk", [P, len(LEVELS) * 64 + P], I32)
        pos = sb("pos", [P, TT], I32)
        posf = sb("posf", [P, TT])
        mods = sb("mods", [P, N_MOD * KD])
        scale_h = sb("scale_h", [P, KD])
        gain_y = sb("gain_y", [P, KD])
        lb = sb("lb", [P, 4, KD])
        csilu = sb("csilu", [P, KD])
        cos = sb("cos", [P, TT, HR])
        sin = sb("sin", [P, TT, HR])
        krT = sb("krT", [ROPE, T])
        stat = sb("stat", [P, 40])
        sums = sb("sums", [P, TT, GD])
        ident = con[:, K_ID:K_ID + P]
        ones = con[:, K_ONE:K_ONE + P]

        PS = ctx.enter_context(nc.psum_tensor("PS", [P, 8, NW], F32))
        XA, XB = 4, 6

        xT = yb[:].rearrange("p a (b c) -> p (a b) c", c=NW)
        prob = dec[:].rearrange("p a b -> p (a b)")[:, 0:3 * NW].rearrange("p (h j s) -> p h j s", h=HPG, j=3)
        rotated = zT[:, 1, 0:NW].rearrange("p (t h d) -> p t h d", t=TT, h=HPG)
        key_weights = v[:].rearrange("p t c -> p (t c)")
        by_rms = stage[:].rearrange("p t c -> p (t c)")[:, 0:TT * P].rearrange("p (t c) -> p t c", t=TT)
        gain_row = zT[:].rearrange("p a b -> p (a b)")
        all_dec = dec[:].rearrange("p a b -> p (a b)")

        def differences(eng, L):
            d = dec[:, L % 2]
            if L == len(LEVELS):
                b = tiles(flat(bT))
                end = b[:, :, 0, P - 1:P].broadcast_to([P, HPG, P])
                return eng.tensor_tensor(tiles(d)[:, :, 0, :], end, b[:, :, 0, :], ALU.subtract)
            m = LEVELS[L]
            b, d = halves(flat(bT), m), halves(d, m)
            end = b[:, :, 0, m - 1:m].broadcast_to([P, HPG * P // m, m])
            eng.tensor_tensor(d[:, :, 1, :], b[:, :, 1, :], end, ALU.subtract)
            return eng.tensor_tensor(d[:, :, 0, :], end, b[:, :, 0, :], ALU.subtract)

        def diagonal(k):
            return (qT, kT)[k // (2 * HPG)][:, k % (2 * HPG)]

        def banks(b):
            return PS[:, b:b + 2, :]

        def by_tile(b):
            return PS[:, b:b + 2, :].rearrange("p b (i s) -> p (b i) s", s=P)

        def by_ktile(b):
            return PS[:, b:b + 2, :].rearrange("p b (k t) -> p (b k) t", t=T)

        def flat_banks(b):
            return PS[:, b:b + 2, :].rearrange("p b c -> p (b c)")

        def gates(j):
            return dec[:, j, :].rearrange("p (t c) -> p t c", t=TT)

        def pairs(t, kp):
            return t[:, 2 * kp:2 * kp + 2, :].rearrange("p k t -> p (k t)")

        def flat(t):
            return t[:].rearrange("p i s -> p (i s)")

        def tiles(f):
            return f.rearrange("p (h two s) -> p h two s", two=2, s=P)

        def halves(f, m):
            return f.rearrange("p (x two m) -> p x two m", two=2, m=m)

        sems = {}

        def sig(name):
            if name not in sems:
                sems[name] = ctx.enter_context(nc.semaphore(name))
            return sems[name]

        raw_loaded = [sig(f"raw_loaded{s}") for s in range(RING)]
        ada_loaded = [sig(f"ada_loaded{s}") for s in range(2)]
        pair_free = [sig("pair_free0"), sig("pair_free1")]
        hi_ready, lo_ready, multiplied = sig("hi_ready"), sig("lo_ready"), sig("multiplied")

        ADA0 = 2 * GD * CD
        QUARTERS = GD
        ADA_Q = ADA0 // QUARTERS
        W_Q = 2 * CD // QUARTERS
        KP_Q = KD // 2 // QUARTERS

        def ada_turns(pl, c):
            return (min(pl.turn(c) + 1, QUARTERS) if pl.chunks == 0 else QUARTERS) * (ADA_Q // RING)

        ADA_STEPS = 2 * GD * KD

        def freed_by(p, groups):
            return (groups - p + 1) // 2

        N_C = 2 * CD
        A_UQ, A_UK, A_UR, A_UV = 0, CL, 2 * CL, 3 * CL
        A_HF = 4 * CL
        A_HQ, A_HI, A_HG = A_HF + CD, A_HF + 2 * CD, A_HF + 3 * CD
        A_OM = A_HF + 4 * CD
        A_OH = A_OM + GD * CR
        A_N = A_OH + GD * CR
        AG = 8 + 2 * GD
        B_GATE = N_C + NG * A_N
        G_GATE = 3 + NG * AG
        B_OUT, G_OUT = B_GATE + GD * 2 * CD, G_GATE + 2 * GD
        B_FF, G_FF = B_OUT + GD * CD, G_OUT + GD
        F_N = 2 * CD + GD * CR
        B_FF1, G_FF1 = B_FF + 2 * CD, G_FF + 2
        B_LAST, G_LAST = B_FF1 + (NF - 1) * F_N, G_FF1 + (NF - 1) * (2 + GD)

        def place_c():
            return Place(0, 0)

        def place_a(g):
            return Place(N_C, 3, A_N, AG, g)

        def place_gate(n):
            return Place(B_GATE, G_GATE, 2 * CD, 2, n)

        def place_out(n):
            return Place(B_OUT, G_OUT, 2 * CD, 2, n)

        def place_ff(n):
            return Place(B_FF1 - F_N, G_FF1 - (2 + GD), F_N, 2 + GD, n)

        ADA_GATE = NG * ADA_A
        ada_step = sig("ada_step")
        A_ADA, G_ADA = 3, 4
        DECAY = [31 + 3 * L // 2 for L in range(len(LEVELS) + 1)]
        LEAD = 2

        block = ctx.enter_context(nc.Block())

        @block.sync
        def _(sp):
            sp.dma_start(vec[:], vectors).then_inc(sig("vectors_loaded"), 16)
            sp.dma_start(pos[:], positions).then_inc(sig("positions_loaded"), 16)
            sp.dma_start(con[:], consts).then_inc(sig("constants_loaded"), 16)
            def load_ada0(c):
                sp.dma_start(raw[:, c % RING], ada0[c]).then_inc(raw_loaded[c % RING], 16)

            for c in range(RING):
                load_ada0(c)
            sp.dma_start(ya[:], x).then_inc(sig("x_loaded"), 16)
            sp.dma_start(key_weights, w_kr).then_inc(sig("kr_loaded"), 16)
            sp.dma_start(msk[:], masks).then_inc(sig("masks_loaded"), 16)
            for n in range(QUARTERS):
                for c in range(0 if n else RING, ADA_Q):
                    if c < RING:
                        sp.wait_ge(lo_ready, (n - 1) * W_Q + c + 1)
                    else:
                        sp.wait_ge(ada_step, (n * ADA_Q + c - RING + 1) * KC)
                    load_ada0(n * ADA_Q + c)
                for c in range(W_Q):
                    sp.wait_ge(ada_step, ((n + 1) * ADA_Q - RING + c + 1) * KC)
                    sp.dma_start(raw[:, c], w_c[n * W_Q + c]).then_inc(raw_loaded[c], 16)

            def load(pl, c, src, width=NW):
                sp.wait_ge(lo_ready, pl.through(c) - RING)
                sp.dma_start(raw[:, pl.slot(c), 0:KC * width], src).then_inc(raw_loaded[pl.slot(c)], 16)

            def load_ada(group, a):
                sp.wait_ge(ada_step, group * KD + (ADA_STEPS + (a - 1) * KC))
                sp.dma_start(ada_raw[:, a % 2], ada1[group * CD + a]).then_inc(ada_loaded[a % 2], 16)

            with sp.Fori(0, NG) as g:
                pl = place_a(g)
                stream = [(w[g, c], NW) for w in (w_uqn, w_uk) for c in range(CL)]
                stream += [(w_uqr[g, c], NW // 2) for c in range(CL)] + [(w_uv[g, c], NW) for c in range(CL)]
                stream += [(w[g, c], NW) for w in (w_hf, w_hq, w_hi, w_hg) for c in range(CD)]
                stream += [(w[g, n, c], NW) for w in (w_omla, w_ohg) for n in range(GD) for c in range(CR)]
                for c, (src, width) in enumerate(stream):
                    load(pl, c, src, width)
                    a = c - A_ADA - LEAD
                    if 0 <= a < ADA_A * CD:
                        load_ada(g * ADA_A + a // CD, a % CD)
            with sp.Fori(0, GD) as n:
                pl = place_gate(n)
                for c in range(2 * CD):
                    load(pl, c, (w_ga if c < CD else w_gb)[n, c % CD])
                    a = c - G_ADA - LEAD
                    if 0 <= a < CD:
                        load_ada(n + ADA_GATE, a)
            with sp.Fori(0, GD // 2) as n:
                pl = place_out(n)
                for c in range(2 * CD):
                    load(pl, c, w_out[n * 2 + c // CD, c % CD])
            sp.wait_ge(sig("gated"), GD)
            sp.dma_start(yb[:], x).then_inc(sig("x_again"), 16)
            first = Place(B_FF, G_FF)
            for c in range(2 * CD):
                load(first, c, (w_gate if c < CD else w_up)[0, c % CD])
            with sp.Fori(1, NF) as n:
                pl = place_ff(n)
                for c in range(CD):
                    load(pl, c, w_gate[n, c])
                for c in range(GD * CR):
                    load(pl, CD + c, w_down[n - 1, c // CR, c % CR])
                for c in range(CD):
                    load(pl, CD + GD * CR + c, w_up[n, c])
            pl = Place(B_LAST, G_LAST)
            for c in range(GD * CR):
                load(pl, c, w_down[NF - 1, c // CR, c % CR])
            for n in range(GD):
                sp.wait_ge(sig("x_final"), TT * (n + 1))
                sp.dma_start(out[:, :, n * NW:(n + 1) * NW], yb[:, :, n * NW:(n + 1) * NW])\
                  .then_inc(sig("stored"), 16)
            sp.wait_ge(sig("stored"), 16 * GD)

        @block.scalar
        def _(act):
            def high(pl, c, width=NW):
                act.wait_ge(raw_loaded[pl.slot(c)], (pl.turn(c) + ada_turns(pl, c) + 1) * 16)
                if not pl.starts(c):
                    act.wait_ge(multiplied, pl.through(c) - RING)
                w = KC * width
                nc.scalar.activation(whi[:, pl.slot(c), 0:w], raw[:, pl.slot(c), 0:w], ACT.Copy)\
                  .then_inc(hi_ready, 1)

            def from_pair(pl, g, c, dst, func=ACT.Copy, free=True, done=None):
                act.wait_ge(multiplied, pl.through(c))
                p = pl.pair(g)
                i = nc.scalar.activation(dst, banks(2 * p), func)
                i.then_inc(pair_free[p] if free else sig(done), 1)

            def square_sum(src, junk, to):
                return nc.scalar.activation(junk, src, ACT.Square, accum_out=to)

            act.wait_ge(sig("vectors_loaded"), 16)
            nc.scalar.activation(csilu[:], vec[:, C_C:C_C + KD], ACT.Sigmoid).then_inc(sig("c_sigmoid"), 1)
            act.wait_ge(sig("x_loaded"), 16)
            for tt in range(TT):
                if tt:
                    act.wait_ge(sig("x_squared"), tt)
                square_sum(ya[:, tt], all_dec, stat[:, tt:tt + 1]).then_inc(sig("x_squared"), 1)
            act.wait_ge(sig("lb_centred"), 2)
            nc.scalar.activation(lb[:, 1:3], lb[:, 1:3], ACT.Exp).then_inc(sig("lb_exp"), 1)
            act.wait_ge(sig("angle_ready"), 1)
            nc.scalar.activation(sin[:].rearrange("p t f -> p (t f)"), stage[:, 0, 0:TT * HR], ACT.Sin).then_inc(sig("sin_ready"), 1)
            nc.scalar.activation(cos[:].rearrange("p t f -> p (t f)"), stage[:, 0, 0:TT * HR], ACT.Sin, scale=0.5).then_inc(sig("sin_ready"), 1)
            act.wait_ge(sig("trunk_rsqrt"), 1)
            for tt in range(TT):
                nc.scalar.activation(ya[:, tt], ya[:, tt], ACT.Copy, scale=stat[:, tt:tt + 1])\
                  .then_inc(sig("x_scaled"), 1)
            for kp in range(KD // 2):
                act.wait_ge(sig("x_transposed"), kp + 1)
                nc.scalar.activation(xT[:, kp], PS[:, kp % 4, :], ACT.Copy).then_inc(sig("xT_copied"), 1)

            pl = place_c()
            for n in range(QUARTERS):
                for c in range(n * W_Q, (n + 1) * W_Q):
                    high(pl, c)
                act.wait_ge(sig("scale_h_ready"), n + 1)
                for k in range(2 * n * KP_Q, 2 * (n + 1) * KP_Q):
                    seg = xT[:, k // 2, k % 2 * T:(k % 2 + 1) * T]
                    act.wait_ge(sig("xT_copied"), k // 2 + 1)
                    nc.scalar.activation(seg, seg, ACT.Identity, scale=scale_h[:, k:k + 1],
                                         bias=mods[:, SH_M + k:SH_M + k + 1]).then_inc(sig("h_scaled"), 1)
                for kp in range(n * KP_Q, (n + 1) * KP_Q):
                    act.wait_ge(sig("h_scaled"), 2 * kp + 2)
                    nc.scalar.activation(pairs(hT_hi, kp), xT[:, kp], ACT.Copy).then_inc(sig("h_high"), 1)
            high(pl, 2 * CD)
            for j, dst in enumerate((stage, side)):
                from_pair(pl, j, 2 * CD - 3 + 2 * j, dst[:])
                act.wait_ge(pair_free[j], 1)
                for tt in range(TT):
                    if tt or j:
                        act.wait_ge(sig("c_squared"), 2 * j + tt)
                    square_sum(dst[:, tt], dec[:, 0, 0:NW], stat[:, 4 + 2 * j + tt:5 + 2 * j + tt])\
                        .then_inc(sig("c_squared"), 1)
                high(pl, 2 * CD + 1 + j)
            for j in range(2):
                act.wait_ge(sig("c_scaled"), 4 * (j + 1))
                nc.scalar.activation(cT_hi[:, j].rearrange("p k t -> p (k t)"), zT[:, j, :], ACT.Copy)\
                  .then_inc(sig("c_high"), 1)
            act.wait_ge(sig("kr_transposed"), 1)
            nc.scalar.activation(krT[:], PS[0:ROPE, XA, 0:T], ACT.Copy).then_inc(sig("krT_copied"), 1)

            with act.Fori(0, NG) as g:
                pl = place_a(g)

                def highs(a, b):
                    for c in range(a, b):
                        high(pl, c, NW // 2 if A_UR <= c < A_UV else NW)

                highs(AHEAD, 5)
                from_pair(pl, 0, A_UK - 1, stage[:])
                highs(5, 7)
                from_pair(pl, 1, A_UR - 1, side[:])
                highs(7, 9)
                act.wait_ge(sig("q_transposed"), g + 1)
                nc.scalar.activation(qT[:], by_tile(XA), ACT.Copy).then_inc(sig("qT_copied"), 1)
                highs(9, 11)
                from_pair(pl, 3, 7, v[:])
                highs(11, 12)
                act.wait_ge(sig("k_transposed"), g + 1)
                nc.scalar.activation(kT[:], by_tile(XB), ACT.Copy).then_inc(sig("kT_copied"), 1)
                highs(12, 13)
                act.wait_ge(sig("qr_transposed"), g + 1)
                nc.scalar.activation(bT[0:ROPE], by_tile(XA)[0:ROPE], ACT.Copy)\
                  .then_inc(sig("qrT_copied"), 1)
                highs(13, 15)
                act.wait_ge(sig("scored"), g + 1)
                nc.scalar.activation(prob[:, :, 1, :], by_tile(XB)[:, 0:HPG], ACT.Copy).then_inc(sig("scores_copied"), 1)
                highs(15, 17)
                act.wait_ge(sig("max_ready"), g + 1)
                for h in range(HPG):
                    for tt in range(TT):
                        cols = prob[:, h, tt:1 + 2 * tt, :]
                        at = tt * HPG + h
                        nc.scalar.activation(cols, cols, ACT.Exp, bias=stat[:, 16 + at:17 + at], scale=SCALE,
                                             accum_out=stat[:, 24 + at:25 + at]).then_inc(sig("exps"), 1)
                highs(17, 20)
                act.wait_ge(sig("p_transposed"), g + 1)
                nc.scalar.activation(pT[:], by_tile(XA), ACT.Copy).then_inc(sig("p_copied"), 1)
                nc.scalar.activation(pTx[:], by_tile(XB)[:, 0:HPG], ACT.Copy).then_inc(sig("p_copied"), 1)
                from_pair(pl, 4, A_HF + CD - 1, stage[:])
                highs(20, 25)
                act.wait_ge(sig("att_transposed"), g + 1)
                nc.scalar.activation(attT_hi[:], by_ktile(XA), ACT.Copy).then_inc(sig("att_high"), 1)
                highs(25, 26)
                act.wait_ge(sig("hf_transposed"), g + 1)
                nc.scalar.activation(kT[:], by_tile(XB), ACT.Sigmoid).then_inc(sig("f_sigmoid"), 1)
                highs(26, 27)
                from_pair(pl, 5, A_HQ + CD - 1, side[:])
                act.wait_ge(sig("f_sigmoid"), g + 1)
                act.wait_ge(sig("lb_step"), 5)
                for h in range(HPG):
                    nc.scalar.activation(bT[:, TT * h:TT * (h + 1), :], kT[:, TT * h:TT * (h + 1), :], ACT.Ln,
                                         scale=lb[:, 2, bass.ds(g * HPG + h, 1)],
                                         bias=lb[:, 1, bass.ds(g * HPG + h, 1)]).then_inc(sig("log_f"), 1)
                highs(27, 28)
                for h in range(HPG):
                    act.wait_ge(sig("log_f"), g * HPG + (h + 1))
                    k = kT[:, TT * h:TT * (h + 1), :]
                    nc.scalar.activation(k, k, ACT.Identity, scale=lb[:, 3, bass.ds(g * HPG + h, 1)],
                                         bias=lb[:, 2, bass.ds(g * HPG + h, 1)]).then_inc(sig("k_ready"), 1)
                highs(28, 29)
                act.wait_ge(sig("hq_transposed"), g + 1)
                nc.scalar.activation(qT[:], by_tile(XA), ACT.Sigmoid).then_inc(sig("q_sigmoid"), 1)
                for c in range(29, A_N + AHEAD):
                    highs(c, c + 1)
                    if c + 1 in DECAY:
                        L = DECAY.index(c + 1)
                        if L == len(LEVELS):
                            act.wait_ge(sig("b_ready"), g * 8 + 8)
                            act.wait_ge(sig("decayed"), g * 8 + (L - 1))
                            nc.scalar.activation(tiles(dec[:, L % 2])[:, :, 1, :], tiles(flat(bT))[:, :, 1, :], ACT.Exp)\
                              .then_inc(sig("decays"), 1)
                        act.wait_ge(sig("diffs"), g * 8 + (L + 1))
                        dif = tiles(dec[:, L % 2])[:, :, 0, :] if L == len(LEVELS) else dec[:, L % 2]
                        nc.scalar.activation(dif, dif, ACT.Exp).then_inc(sig("decays"), 1)
                    if c == A_HG + 3:
                        from_pair(pl, 6, A_HG - 1, v[:])
                    if c == DECAY[-1] + 1:
                        act.wait_ge(sig("cross_scored"), g + 1)
                        nc.scalar.activation(pTx[:], by_tile(XB)[:, HPG:], ACT.Copy).then_inc(sig("cross_copied"), 1)
                    if c == A_OM + 2:
                        from_pair(pl, 7, A_OM - 1, side[:], ACT.Sigmoid, False, "og_sigmoid")
                    if c == A_OH - 4:
                        act.wait_ge(sig("o_summed"), g + 1)
                        nc.scalar.activation(dec[:, 0, :], flat_banks(XB), ACT.Square).then_inc(sig("o_squared"), 1)
                    if c == A_OH:
                        act.wait_ge(sig("o_transposed"), g + 1)
                        nc.scalar.activation(oT_hi[:], by_ktile(XA), ACT.Copy).then_inc(sig("o_high"), 1)

            with act.Fori(0, GD) as n:
                pl = place_gate(n)
                for c in range(AHEAD, CD + 3):
                    high(pl, c)
                from_pair(pl, 0, CD - 1, gates(0), ACT.Sigmoid)
                for c in range(CD + 3, 2 * CD + AHEAD):
                    high(pl, c)
                from_pair(pl, 1, 2 * CD - 1, gates(1), ACT.Sigmoid)

            act.wait_ge(sig("gain_spread"), 1)
            for i in range(2):
                nc.scalar.activation(zT[:, i], flat_banks(XA + 2 * i), ACT.Copy).then_inc(sig("gain_copied"), 1)
            for kp in range(KD // 2):
                act.wait_ge(sig("m_transposed"), kp + 1)
                nc.scalar.activation(pairs(hT_hi, kp), PS[:, XA + kp % 4, :], ACT.Copy)\
                  .then_inc(sig("m_high"), 1)

            with act.Fori(0, GD // 2) as n:
                pl = place_out(n)
                for j in range(2):
                    for c in range(j * CD + AHEAD, (j + 1) * CD + AHEAD):
                        high(pl, c)
                    act.wait_ge(multiplied, pl.through((j + 1) * CD - 1))
                    for tt in range(TT):
                        if j or tt:
                            act.wait_ge(sig("y_squared"), n * (2 * TT) + (j * TT + tt))
                        nc.scalar.activation(dec[:, 0, 0:NW], PS[:, 2 * pl.pair(j) + tt, :], ACT.Square,
                                             accum_out=sums[:, tt, bass.ds(n * 2 + j, 1)])\
                          .then_inc(sig("y_squared"), 1)
            for tt in range(TT):
                act.wait_ge(sig("x_mixed"), tt + 1)
                if tt:
                    act.wait_ge(sig("x2_squared"), tt)
                square_sum(yb[:, tt], all_dec, stat[:, 10 + tt:11 + tt]).then_inc(sig("x2_squared"), 1)
            first = Place(B_FF, G_FF)
            for kp in range(KD // 2):
                if kp == 0 or kp > AHEAD:
                    high(first, max(kp, AHEAD))
                act.wait_ge(sig("h2_scaled"), 2 * kp + 2)
                nc.scalar.activation(pairs(hT_hi, kp), dec[:, kp % 2, 0:NW], ACT.Copy)\
                  .then_inc(sig("h2_high"), 1)

            def hidden_high(n):
                act.wait_ge(sig("ff_transposed"), n)
                nc.scalar.activation(oT_hi[:], by_ktile(XA), ACT.Copy).then_inc(sig("ff_high"), 1)

            for c in range(CD, CD + 3):
                high(first, c)
            from_pair(first, 0, CD - 1, stage[:], ACT.Sigmoid, False, "ff_sigmoid")
            for c in range(CD + 3, 2 * CD):
                high(first, c)
            with act.Fori(1, NF) as n:
                pl = place_ff(n)
                for c in range(7):
                    high(pl, c)
                hidden_high(n)
                for c in range(7, CD + 3):
                    high(pl, c)
                from_pair(pl, 0, CD - 1, stage[:], ACT.Sigmoid, False, "ff_sigmoid")
                for c in range(CD + 3, F_N):
                    high(pl, c)
            pl = Place(B_LAST, G_LAST)
            for c in range(RING):
                high(pl, c)
            hidden_high(NF)
            for c in range(RING, GD * CR):
                high(pl, c)
            for n in range(GD):
                p = (G_LAST + n) % 2
                act.wait_ge(pair_free[p], freed_by(p, G_LAST + n + 1))
                for tt in range(TT):
                    if n or tt:
                        act.wait_ge(sig("y2_squared"), n * TT + tt)
                    square_sum(ya[:, tt, n * NW:(n + 1) * NW], dec[:, 0, 0:NW], sums[:, tt, n:n + 1])\
                        .then_inc(sig("y2_squared"), 1)

        @block.gpsimd
        def _(pool):
            def power(src, width, name, count=0):
                pool.wait_ge(sig(name + "_mean"), count + 1)
                nc.gpsimd.tensor_tensor(src, src, con[:, K_POW:K_POW + width], ALU.pow)\
                  .then_inc(sig(name + "_rsqrt"), 1)

            pool.wait_ge(sig("constants_loaded"), 16)
            power(stat[:, 0:TT], TT, "trunk")
            pool.wait_ge(sig("x_transposed"), KD // 2)
            nc.gpsimd.memset(ya[:], 0.0).then_inc(sig("sums_zeroed"), 1)
            for j in range(2):
                power(stat[:, 4 + 2 * j:6 + 2 * j], TT, "c", j)
            pool.wait_ge(sig("kr_multiplied"), 1)
            nc.gpsimd.memset(yb[:], 0.0).then_inc(sig("sums_zeroed"), 1)
            with pool.Fori(0, NG) as g:
                for L in range(len(LEVELS) + 1):
                    if L == 0:
                        pool.wait_ge(sig("b_ready"), g * 8 + 8)
                    if L >= 2:
                        pool.wait_ge(sig("decayed"), g * 8 + (L - 1))
                    differences(nc.gpsimd, L).then_inc(sig("diffs"), 1)
                power(stat[:, 32:40], TT * HPG, "o", g)
            power(stat[:, 8:8 + TT], TT, "trunk", 1)
            pool.wait_ge(sig("x_mixed"), TT)
            power(stat[:, 10:10 + TT], TT, "trunk", 2)
            nc.gpsimd.memset(ya[:], 0.0).then_inc(sig("sums_zeroed"), 1)
            power(stat[:, 12:12 + TT], TT, "trunk", 3)

        @block.tensor
        def _(pe):
            def multiply(pl, g, n, c0, a, b, hi, lo, width=NW, kt0=0):
                p = pl.pair(g)
                for c in range(a, b):
                    if c == 0 and not pl.fresh(g):
                        pe.wait_ge(pair_free[p], pl.freed(g))
                    pe.wait_ge(lo_ready, pl.through(c0 + c))
                    s = pl.slot(c0 + c)
                    for tt in range(TT):
                        for k in range(KC):
                            kt = kt0 + c * KC + k
                            tok = slice(tt * P, (tt + 1) * P)
                            cols = slice(k * width, (k + 1) * width)
                            o = PS[:, 2 * p + tt, 0:width]
                            start, stop = c == 0 and k == 0, c == n - 1 and k == KC - 1
                            nc.tensor.matmul(o, hi[:, kt, tok], whi[:, s, cols], start=start, stop=False)
                            nc.tensor.matmul(o, hi[:, kt, tok], wlo[:, s, cols], start=False, stop=False)
                            last = nc.tensor.matmul(o, lo[:, kt, tok], whi[:, s, cols], start=False, stop=stop)
                    last.then_inc(multiplied, 1)

            def transpose_group(src, bank):
                for h in range(HPG):
                    for tt in range(TT):
                        last = nc.tensor.transpose(PS[:, bank + h // 2, ((h % 2) * TT + tt) * P:][:, 0:P],
                                                   src[:, tt, h * P:(h + 1) * P], ident)
                return last

            def transpose_pair(src, kp, bank):
                for j in range(2):
                    for tt in range(TT):
                        k = 2 * kp + j
                        last = nc.tensor.transpose(PS[:, bank, (j * TT + tt) * P:][:, 0:P],
                                                   src[:, tt, k * P:(k + 1) * P], ident)
                return last

            def attend():
                for h in range(HPG):
                    cols = slice(h * P, (h + 1) * P)
                    nc.tensor.matmul(PS[:, XB, cols], pT[:, 2 * h], v[:, 0, cols], start=True, stop=True)
                    nc.tensor.matmul(PS[:, XB + 1, cols], pTx[:, h], v[:, 0, cols], start=True, stop=False)
                    last = nc.tensor.matmul(PS[:, XB + 1, cols], pT[:, 2 * h + 1], v[:, 1, cols],
                                            start=False, stop=True)
                return last

            def sum_rows(acc, bank, at=0):
                for j in range(NW // P):
                    last = nc.tensor.matmul(PS[:, bank, at + j:at + j + 1], acc[:, j * P:(j + 1) * P], ones[:, 0:1],
                                            start=True, stop=True)
                return last

            pe.wait_ge(sig("constants_loaded"), 16)
            pe.wait_ge(sig("x_scaled"), TT)
            for kp in range(KD // 2):
                if kp >= 4:
                    pe.wait_ge(sig("xT_copied"), kp - 3)
                transpose_pair(ya, kp, kp % 4).then_inc(sig("x_transposed"), 1)
            pl = place_c()
            pe.wait_ge(sig("xT_copied"), KD // 2)
            for n in range(QUARTERS):
                for q in range(2 * n, 2 * n + 2):
                    pe.wait_ge(ada_step, KD * (q + 1))
                    sum_rows(ada_acc[:, q % 2], XA, q * (NW // P)).then_inc(sig("ada0_summed"), 1)
                pe.wait_ge(sig("h_low"), (n + 1) * KP_Q)
                for j in range(2):
                    multiply(pl, j, CD, 2 * n + 2 * j, 2 * n, 2 * n + 2, hT_hi, hT_lo)

            pe.wait_ge(sig("c_normed"), TT)
            transpose_group(stage, XA).then_inc(sig("c_transposed"), 1)
            pe.wait_ge(pair_free[pl.pair(2)], pl.freed(2))
            pe.wait_ge(sig("kr_loaded"), 16)
            for tt in range(TT):
                for k in range(KD):
                    o = PS[:, 2 * pl.pair(2) + tt, 0:ROPE]
                    at = (k % 2) * T + tt * P
                    last = nc.tensor.matmul(o, xT[:, k // 2, at:at + P], key_weights[:, k * ROPE:(k + 1) * ROPE],
                                            start=k == 0, stop=k == KD - 1)
            last.then_inc(sig("kr_multiplied"), 1)
            pe.wait_ge(sig("c_normed"), 2 * TT)
            transpose_group(side, XB).then_inc(sig("c_transposed"), 1)
            pe.wait_ge(sig("kr_rotated"), 1)
            pe.wait_ge(sig("c_scaled"), 4)
            for tt in range(TT):
                last = nc.tensor.transpose(PS[0:ROPE, XA, tt * P:(tt + 1) * P],
                                           qT[:, tt, 0:ROPE], ident)
            last.then_inc(sig("kr_transposed"), 1)

            with pe.Fori(0, NG) as g:
                pl = place_a(g)

                def hf(a, b):
                    multiply(pl, 4, CD, A_HF, a - A_HF, b - A_HF, hT_hi, hT_lo)

                def hq(a, b):
                    multiply(pl, 5, CD, A_HQ, a - A_HQ, b - A_HQ, hT_hi, hT_lo)

                def after_hq(c):
                    if c < A_HG:
                        multiply(pl, 6, CD, A_HI, c - A_HI, c + 1 - A_HI, hT_hi, hT_lo)
                    elif c < A_OM:
                        multiply(pl, 7, CD, A_HG, c - A_HG, c + 1 - A_HG, hT_hi, hT_lo)
                    else:
                        n, k = (c - A_OM) // CR, (c - A_OM) % CR
                        multiply(pl, 8 + n, CR, A_OM + n * CR, k, k + 1, attT_hi, attT_lo)

                pe.wait_ge(sig("c_low"), 1)
                multiply(pl, 0, CL, A_UQ, 0, CL, cT_hi[:, 0], cT_lo[:, 0])
                pe.wait_ge(sig("c_low"), 2)
                multiply(pl, 1, CL, A_UK, 0, CL, cT_hi[:, 1], cT_lo[:, 1])
                multiply(pl, 2, CL, A_UR, 0, CL, cT_hi[:, 0], cT_lo[:, 0], NW // 2)
                pe.wait_ge(sig("krT_copied"), 1)
                pe.wait_ge(pair_free[pl.pair(0)], pl.freed(0) + 1)
                transpose_group(stage, XA).then_inc(sig("q_transposed"), 1)
                multiply(pl, 3, CL, A_UV, 0, CL, cT_hi[:, 1], cT_lo[:, 1])
                hf(8, 9)
                pe.wait_ge(pair_free[pl.pair(1)], pl.freed(1) + 1)
                transpose_group(side, XB).then_inc(sig("k_transposed"), 1)
                pe.wait_ge(sig("qT_copied"), g + 1)
                hf(9, 10)
                pe.wait_ge(sig("constants_loaded"), 16)
                pe.wait_ge(sig("qr_rotated"), g + 1)
                for h in range(HPG):
                    for tt in range(TT):
                        last = nc.tensor.transpose(PS[0:ROPE, XA + h // 2, ((h % 2) * TT + tt) * P:][:, 0:P],
                                                   rotated[:, tt, h, :], ident)
                last.then_inc(sig("qr_transposed"), 1)
                hf(10, 12)
                pe.wait_ge(sig("kT_copied"), g + 1)
                pe.wait_ge(sig("qrT_copied"), g + 1)
                for h in range(HPG):
                    for tt, s, o in ((0, 0, PS[:, XA + h // 2, (h % 2) * 2 * P:][:, 0:P]),
                                     (1, 1, PS[:, XA + h // 2, (h % 2) * 2 * P + P:][:, 0:P]),
                                     (1, 0, PS[:, XB, h * P:(h + 1) * P])):
                        nc.tensor.matmul(o, qT[:, 2 * h + tt], kT[:, 2 * h + s], start=True, stop=False)
                        last = nc.tensor.matmul(o, bT[0:ROPE, 2 * h + tt], krT[:, s * P:(s + 1) * P],
                                                start=False, stop=True)
                last.then_inc(sig("scored"), 1)
                pe.wait_ge(ada_step, g * (ADA_A * KD) + (ADA_STEPS + KD))
                sum_rows(ada_acc[:, 0], XB + 1).then_inc(sig("ada_summed_a"), 1)
                hf(12, 16)
                hq(16, 17)
                pe.wait_ge(sig("exps"), g * 8 + 8)
                for h in range(HPG):
                    for tt in range(TT):
                        nc.tensor.transpose(PS[:, XA + h // 2, ((h % 2) * TT + tt) * P:][:, 0:P],
                                            prob[:, h, 2 * tt, :], ident)
                    last = nc.tensor.transpose(PS[:, XB, h * P:(h + 1) * P], prob[:, h, 1, :], ident)
                last.then_inc(sig("p_transposed"), 1)
                hq(17, 20)
                pe.wait_ge(sig("p_copied"), g * 2 + 2)
                pe.wait_ge(sig("mods_a"), g + 1)
                attend().then_inc(sig("att_summed"), 1)
                pe.wait_ge(ada_step, g * (ADA_A * KD) + (ADA_STEPS + 2 * KD))
                sum_rows(ada_acc[:, 1], XA).then_inc(sig("ada_summed_b"), 1)
                hq(20, 22)
                pe.wait_ge(sig("mods_b"), g + 1)
                pe.wait_ge(sig("att_scaled"), g + 1)
                transpose_group(side, XA).then_inc(sig("att_transposed"), 1)
                hq(22, 23)
                pe.wait_ge(pair_free[pl.pair(4)], pl.freed(4) + 1)
                transpose_group(stage, XB).then_inc(sig("hf_transposed"), 1)
                hq(23, 24)
                after_hq(24)
                after_hq(25)
                pe.wait_ge(sig("att_low"), g + 1)
                pe.wait_ge(pair_free[pl.pair(5)], pl.freed(5) + 1)
                transpose_group(side, XA).then_inc(sig("hq_transposed"), 1)
                for c in range(26, A_OH):
                    after_hq(c)
                    if c == DECAY[0] - 2:
                        pe.wait_ge(sig("q_ready"), g + 1)
                        pe.wait_ge(sig("k_ready"), g * HPG + HPG)
                        for i in range(2 * HPG):
                            last = nc.tensor.matmul(PS[:, XB + i // 4, (i % 4) * P:][:, 0:P], kT[:, i], qT[:, i],
                                                    start=True, stop=True)
                        last.then_inc(sig("self_scored"), 1)
                    if c + 2 in DECAY[:-1]:
                        L = DECAY.index(c + 2)
                        m = LEVELS[L]
                        pe.wait_ge(sig("decayed"), g * 8 + (L + 1))
                        if L >= 2:
                            pe.wait_ge(sig("self_merged"), g + 1)
                        if L >= 4:
                            pe.wait_ge(sig(f"level{L - 4}_merged"), g + 1)
                        z = zT[:, L % 2].rearrange("p (i s) -> p i s", s=P)
                        zt = zT[:, L % 2].rearrange("p (i x two m) -> p i x two m", i=2 * HPG, two=2, m=m)
                        for i in range(2 * HPG):
                            last = nc.tensor.matmul(PS[:, XA + L % 4, i * 64:(i + 1) * 64], z[:, i],
                                                    zt[:, i, :, 1, :], start=True, stop=True)
                        last.then_inc(sig(f"level{L}_scored"), 1)
                    if c + 2 == DECAY[-1]:
                        L = len(LEVELS)
                        pe.wait_ge(sig("decayed"), g * 8 + (L + 1))
                        pe.wait_ge(sig(f"level{L - 4}_merged"), g + 1)
                        for h in range(HPG):
                            z = zT[:, L % 2].rearrange("p (i s) -> p i s", s=P)
                            last = nc.tensor.matmul(PS[:, XB + 1, h * P:(h + 1) * P], z[:, 2 * h], z[:, 2 * h + 1],
                                                    start=True, stop=True)
                        last.then_inc(sig("cross_scored"), 1)
                    if c == DECAY[-1]:
                        pe.wait_ge(sig(f"level{len(LEVELS) - 1}_merged"), g + 1)
                        pe.wait_ge(sig("cross_copied"), g + 1)
                        attend().then_inc(sig("o_summed"), 1)
                    if c == A_OH - 3:
                        pe.wait_ge(sig("o_gated"), g + 1)
                        transpose_group(stage, XA).then_inc(sig("o_transposed"), 1)
                        pe.wait_ge(ada_step, g * (ADA_A * KD) + (ADA_STEPS + 3 * KD))
                        sum_rows(ada_acc[:, 0], XB + 1).then_inc(sig("ada_summed_c"), 1)
                pe.wait_ge(sig("o_low"), g + 1)
                for n in range(GD):
                    multiply(pl, 8 + GD + n, CR, A_OH + n * CR, 0, CR, oT_hi, oT_lo)

            with pe.Fori(0, GD) as n:
                pl = place_gate(n)
                multiply(pl, 0, CD, 0, 0, CD, hT_hi, hT_lo)
                multiply(pl, 1, CD, CD, 0, CD - 1, hT_hi, hT_lo)
                pe.wait_ge(ada_step, n * KD + (ADA_STEPS + ADA_GATE * KD + KD))
                pe.wait_ge(sig("mods_c"), NG)
                sum_rows(ada_acc[:, 0], XB + 1).then_inc(sig("ada_summed_d"), 1)
                multiply(pl, 1, CD, CD, CD - 1, CD, hT_hi, hT_lo)

            def spread_gain(which):
                pe.wait_ge(sig("gain_diagonal"), which * KD)
                for k in range(KD):
                    last = nc.tensor.matmul(PS[:, XA + k // 4, (k % 4) * P:][:, 0:P], ones,
                                            diagonal(k),
                                            start=True, stop=True)
                last.then_inc(sig("gain_spread"), 1)

            pe.wait_ge(sig("mods_d"), GD)
            spread_gain(1)
            for kp in range(KD // 2):
                if kp < 4:
                    pe.wait_ge(sig("gain_copied"), kp // 2 + 1)
                else:
                    pe.wait_ge(sig("m_low"), kp - 3)
                pe.wait_ge(sig("gated"), kp // 2 + 1)
                transpose_pair(ya, kp, XA + kp % 4).then_inc(sig("m_transposed"), 1)
            with pe.Fori(0, GD // 2) as n:
                pl = place_out(n)
                for j in range(2):
                    for c in range(CD):
                        if j == 0:
                            pe.wait_ge(sig("m_low"), c + 1)
                        multiply(pl, j, CD, j * CD, c, c + 1, hT_hi, hT_lo)

            for kp in range(KD // 2):
                if kp >= 4:
                    pe.wait_ge(sig("h2_scaled"), 2 * (kp - 3))
                for j in range(2):
                    for tt in range(TT):
                        if kp == 0 and j == 0:
                            pe.wait_ge(sig("rms_diagonal"), tt + 1)
                        k = 2 * kp + j
                        last = nc.tensor.matmul(PS[:, XA + kp % 4, (j * TT + tt) * P:][:, 0:P],
                                                yb[:, tt, k * P:(k + 1) * P], by_rms[:, tt], start=True, stop=True)
                last.then_inc(sig("x2_transposed"), 1)

            first = Place(B_FF, G_FF)
            for c in range(CD):
                pe.wait_ge(sig("h2_low"), c + 1)
                multiply(first, 0, CD, 0, c, c + 1, hT_hi, hT_lo)
            multiply(first, 1, CD, CD, 0, CD, hT_hi, hT_lo)

            def hidden_transposed(pl):
                pe.wait_ge(pair_free[pl.pair(-1)], pl.freed(-1) + 1)
                transpose_group(stage, XA).then_inc(sig("ff_transposed"), 1)

            with pe.Fori(1, NF) as n:
                pl = place_ff(n)
                multiply(pl, 0, CD, 0, 0, 4, hT_hi, hT_lo)
                hidden_transposed(pl)
                multiply(pl, 0, CD, 0, 4, CD, hT_hi, hT_lo)
                pe.wait_ge(sig("ff_low"), n)
                for j in range(GD):
                    multiply(pl, 1 + j, CR, CD + j * CR, 0, CR, oT_hi, oT_lo)
                multiply(pl, 1 + GD, CD, CD + GD * CR, 0, CD, hT_hi, hT_lo)
            pl = Place(B_LAST, G_LAST)
            hidden_transposed(pl)
            pe.wait_ge(sig("ff_low"), NF)
            for j in range(GD):
                if j == GD - 1:
                    spread_gain(2)
                multiply(pl, j, CR, j * CR, 0, CR, oT_hi, oT_lo)

        @block.vector
        def _(dve):
            def low(pl, c, width=NW):
                dve.wait_ge(hi_ready, pl.through(c))
                w = KC * width
                s = pl.slot(c)
                nc.vector.tensor_tensor(wlo[:, s, 0:w], raw[:, s, 0:w], whi[:, s, 0:w].bitcast(F32), ALU.subtract)\
                  .then_inc(lo_ready, 1)

            def ada_chunk(group, a, j):
                dve.wait_ge(ada_loaded[a % 2], (group * (CD // 2) + (a // 2 + 1)) * 16)
                for k in range(KC):
                    at = a * KC + k
                    part = ada_raw[:, a % 2, k * NW:(k + 1) * NW]
                    if at == 0:
                        last = nc.vector.tensor_scalar(ada_acc[:, j], part, csilu[:, 0:1], None, ALU.mult)
                    else:
                        dve.wait_ge(ada_step, group * KD + (ADA_STEPS + at))
                        last = nc.vector.scalar_tensor_tensor(
                            out=ada_acc[:, j], in0=part, scalar=csilu[:, at:at + 1], in1=ada_acc[:, j],
                            op0=ALU.mult, op1=ALU.add)
                    last.then_inc(ada_step, 1)

            def piece(group, name):
                at = group * (NW // P)
                nc.vector.tensor_tensor(mods[:, bass.ds(at + 2 * KD, NW // P)], PS[:, XA if name == "b" else XB + 1, 0:NW // P],
                                        vec[:, bass.ds(at + (C_BADA + 2 * KD), NW // P)], ALU.add)\
                  .then_inc(sig("mods_" + name), 1)

            dve.wait_ge(sig("vectors_loaded"), 16)
            dve.wait_ge(sig("c_sigmoid"), 1)
            nc.vector.tensor_tensor(csilu[:], csilu[:], vec[:, C_C:C_C + KD], ALU.mult).then_inc(sig("c_silu"), 1)
            l0, l1 = vec[:, C_LB:C_LB + KD], vec[:, C_LB + KD:C_LB + 2 * KD]
            nc.vector.tensor_tensor(lb[:, 0], l0, l1, ALU.max).then_inc(sig("lb_max"), 1)
            dve.wait_ge(sig("lb_max"), 1)
            nc.vector.tensor_tensor(lb[:, 1], l0, lb[:, 0], ALU.subtract).then_inc(sig("lb_centred"), 1)
            nc.vector.tensor_tensor(lb[:, 2], l1, lb[:, 0], ALU.subtract).then_inc(sig("lb_centred"), 1)
            dve.wait_ge(sig("constants_loaded"), 16)
            dve.wait_ge(sig("positions_loaded"), 16)
            nc.vector.tensor_copy(posf[:], pos[:]).then_inc(sig("pos_float"), 1)
            dve.wait_ge(sig("pos_float"), 1)
            ang, turns = stage[:, 0, 0:TT * HR], stage[:, 0, TT * HR:2 * TT * HR]
            for tt in range(TT):
                nc.vector.tensor_scalar(ang[:, tt * HR:(tt + 1) * HR], con[:, K_FREQ:K_FREQ + HR],
                                        posf[:, tt:tt + 1], None, ALU.mult).then_inc(sig("angle_step"), 1)
            dve.wait_ge(sig("angle_step"), 2)
            nc.vector.tensor_scalar(turns, ang, 1.0 / 6.283185307179586, ROUND, ALU.mult, ALU.add)\
              .then_inc(sig("angle_step"), 1)
            dve.wait_ge(sig("angle_step"), 3)
            nc.vector.tensor_scalar(turns, turns, -ROUND, None, ALU.add).then_inc(sig("angle_step"), 1)
            for i, part in enumerate((TWO_PI_HI, TWO_PI_MID, TWO_PI_LO)):
                dve.wait_ge(sig("angle_step"), 4 + i)
                nc.vector.scalar_tensor_tensor(out=ang, in0=turns, scalar=-part, in1=ang, op0=ALU.mult, op1=ALU.add)\
                  .then_inc(sig("angle_step"), 1)
            dve.wait_ge(sig("angle_step"), 7)
            nc.vector.tensor_scalar(ang, ang, 3.1415925, -3.1415925, ALU.min, ALU.max).then_inc(sig("angle_ready"), 1)
            def rsqrt_of(src, n, name, count=0, between=None):
                nc.vector.tensor_scalar(src, src, 1.0 / n, EPS, ALU.mult, ALU.add).then_inc(sig(name + "_mean"), 1)
                if between:
                    between()
                dve.wait_ge(sig(name + "_rsqrt"), count + 1)

            dve.wait_ge(sig("c_silu"), 1)

            def shift_and_scale(n):
                w = NW // P
                dve.wait_ge(sig("ada0_summed"), 2 * (n + 1))
                nc.vector.tensor_tensor(
                    mods[:, 0:2 * KD].rearrange("p (a k) -> p a k", a=2)[:, :, n * w:(n + 1) * w],
                    PS[:, XA, 2 * n * w:2 * (n + 1) * w].rearrange("p (a k) -> p a k", a=2),
                    vec[:, C_BADA:C_BADA + 2 * KD].rearrange("p (a k) -> p a k", a=2)[:, :, n * w:(n + 1) * w],
                    ALU.add).then_inc(sig("mods0"), 1)
                dve.wait_ge(sig("mods0"), n + 1)
                nc.vector.scalar_tensor_tensor(
                    out=scale_h[:, n * w:(n + 1) * w], in0=mods[:, SC_M + n * w:SC_M + (n + 1) * w], scalar=1.0,
                    in1=vec[:, C_GPRE + n * w:C_GPRE + (n + 1) * w], op0=ALU.add, op1=ALU.mult)\
                  .then_inc(sig("scale_h_ready"), 1)

            def quarter_low(n):
                for kp in range(n * KP_Q, (n + 1) * KP_Q):
                    dve.wait_ge(sig("h_high"), kp + 1)
                    nc.vector.tensor_tensor(pairs(hT_lo, kp), xT[:, kp], pairs(hT_hi, kp).bitcast(F32),
                                            ALU.subtract).then_inc(sig("h_low"), 1)

            def first_groups(n, j):
                q = 2 * n + j
                if n:
                    dve.wait_ge(sig("ada0_summed"), q - 1)
                for at in range(KD):
                    c, k = j * CD + at // KC, at % KC
                    part = raw[:, c % RING, k * NW:(k + 1) * NW]
                    if k == 0:
                        turn = n * (ADA_Q // RING + 1) + c // RING
                        dve.wait_ge(raw_loaded[c % RING], (turn + 1) * 16)
                    if at == 0:
                        last = nc.vector.tensor_scalar(ada_acc[:, j], part, csilu[:, 0:1], None, ALU.mult)
                    else:
                        dve.wait_ge(ada_step, q * KD + at)
                        last = nc.vector.scalar_tensor_tensor(
                            out=ada_acc[:, j], in0=part, scalar=csilu[:, at:at + 1], in1=ada_acc[:, j],
                            op0=ALU.mult, op1=ALU.add)
                    last.then_inc(ada_step, 1)
                    if n and j == 0 and at == 1:
                        shift_and_scale(n - 1)
                    if n and j == 0 and at == 5:
                        quarter_low(n - 1)
                    if q == 0 and at == 3 * KD // 4:
                        dve.wait_ge(sig("x_squared"), TT)
                        nc.vector.tensor_scalar(stat[:, 0:TT], stat[:, 0:TT], 1.0 / D, EPS, ALU.mult, ALU.add)\
                          .then_inc(sig("trunk_mean"), 1)

            def tables():
                dve.wait_ge(sig("sin_ready"), 2)
                nc.vector.tensor_tensor(cos[:], cos[:], cos[:], ALU.mult).then_inc(sig("cos_square"), 1)
                dve.wait_ge(sig("cos_square"), 1)
                nc.vector.tensor_scalar(cos[:], cos[:], -2.0, 1.0, ALU.mult, ALU.add).then_inc(sig("cos_ready"), 1)
                dve.wait_ge(sig("lb_exp"), 1)
                nc.vector.tensor_tensor(lb[:, 3], lb[:, 1], lb[:, 2], ALU.add).then_inc(sig("lb_step"), 1)
                dve.wait_ge(sig("lb_step"), 1)
                nc.vector.reciprocal(lb[:, 3], lb[:, 3]).then_inc(sig("lb_step"), 1)
                dve.wait_ge(sig("lb_step"), 2)
                nc.vector.tensor_tensor(lb[:, 1], lb[:, 1], lb[:, 3], ALU.mult).then_inc(sig("lb_step"), 1)
                dve.wait_ge(sig("lb_step"), 3)
                nc.vector.tensor_scalar(lb[:, 2], lb[:, 1], -1.0, 1.0, ALU.mult, ALU.add).then_inc(sig("lb_step"), 1)
                nc.vector.tensor_scalar(lb[:, 3], lb[:, 1], 1.0, -1.0, ALU.mult, ALU.add).then_inc(sig("lb_step"), 1)

            pl = place_c()
            for n in range(QUARTERS):
                for j in range(2):
                    first_groups(n, j)
                    if n == 0 and j == 0:
                        tables()
                split = (n + 1) * W_Q - (2 if n == QUARTERS - 1 else 0)
                for c in range(n * W_Q, split):
                    low(pl, c)
                if n == QUARTERS - 1:
                    shift_and_scale(n)
                    quarter_low(n)
                for c in range(split, (n + 1) * W_Q):
                    low(pl, c)

            def normed(j, src):
                dve.wait_ge(sig("c_squared"), 2 * (j + 1))
                rsqrt_of(stat[:, 4 + 2 * j:6 + 2 * j], LORA, "c", j)
                for tt in range(TT):
                    nc.vector.tensor_scalar(src[:, tt], src[:, tt], stat[:, 4 + 2 * j + tt:5 + 2 * j + tt], None,
                                            ALU.mult).then_inc(sig("c_normed"), 1)

            def gained(j):
                dve.wait_ge(sig("c_transposed"), j + 1)
                for k in range(LORA // P):
                    gain = vec[:, C_GQ + j * (LORA // P) + k:][:, 0:1]
                    nc.vector.tensor_scalar(zT[:, j, k * T:(k + 1) * T], by_ktile(XA if j == 0 else XB)[:, k], gain,
                                            None, ALU.mult).then_inc(sig("c_scaled"), 1)

            def compressed_low(j):
                dve.wait_ge(sig("c_high"), j + 1)
                nc.vector.tensor_tensor(cT_lo[:, j].rearrange("p k t -> p (k t)"), zT[:, j],
                                        cT_hi[:, j].rearrange("p k t -> p (k t)").bitcast(F32),
                                        ALU.subtract).then_inc(sig("c_low"), 1)

            def rotate(src, dst, parts, heads, free, done, count):
                a, b = src[:, :, :, 0:HR], src[:, :, :, HR:ROPE]
                co = cos[:].unsqueeze(2).broadcast_to([P, TT, heads, HR])
                si = sin[:].unsqueeze(2).broadcast_to([P, TT, heads, HR])
                n = TT * heads * HR
                pr = [parts[:, i * n:(i + 1) * n].rearrange("p (t h d) -> p t h d", t=TT, h=heads) for i in range(4)]
                nc.vector.tensor_tensor(pr[0], a, co, ALU.mult)
                nc.vector.tensor_tensor(pr[1], b, si, ALU.mult)
                nc.vector.tensor_tensor(pr[2], b, co, ALU.mult)
                nc.vector.tensor_tensor(pr[3], a, si, ALU.mult).then_inc(free[0], 1)
                dve.wait_ge(free[0], free[1] + 1)
                nc.vector.tensor_tensor(dst[:, :, :, 0:HR], pr[0], pr[1], ALU.subtract)
                nc.vector.tensor_tensor(dst[:, :, :, HR:ROPE], pr[2], pr[3], ALU.add).then_inc(sig(done), 1)

            def add_pair(pl, g, c, dst):
                dve.wait_ge(multiplied, pl.through(c))
                p = pl.pair(g)
                nc.vector.tensor_tensor(dst, dst, banks(2 * p), ALU.add).then_inc(pair_free[p], 1)

            low(pl, 2 * CD)
            normed(0, stage)
            low(pl, 2 * CD + 1)
            gained(0)
            normed(1, side)
            low(pl, 2 * CD + 2)
            compressed_low(0)
            dve.wait_ge(sig("kr_multiplied"), 1)
            dve.wait_ge(sig("cos_ready"), 1)
            rotate(PS[:, 0:2, 0:ROPE].unsqueeze(2), qT[:, 0:TT, 0:ROPE].unsqueeze(2), flat(kT), 1,
                   (pair_free[0], 1), "kr_rotated", 0)
            gained(1)
            compressed_low(1)

            with dve.Fori(0, NG) as g:
                pl = place_a(g)

                def steps(a, b):
                    for c in range(a, b):
                        low(pl, c, NW // 2 if A_UR <= c < A_UV else NW)
                        i = c - A_ADA
                        if 0 <= i < ADA_A * CD:
                            j = i // CD
                            if i == 2 * CD:
                                dve.wait_ge(sig("ada_summed_a"), g + 1)
                            ada_chunk(g * ADA_A + j, i % CD, j % 2)

                steps(AHEAD, 8)
                dve.wait_ge(multiplied, pl.through(A_UV - 1))
                p = pl.pair(2)
                rotate(PS[:, 2 * p:2 * p + 2, 0:NW // 2].rearrange("p t (h d) -> p t h d", h=HPG), rotated,
                       zT[:, 0], HPG, (pair_free[p], pl.freed(2)), "qr_rotated", g)
                steps(8, 15)
                dve.wait_ge(sig("scored"), g + 1)
                nc.vector.tensor_tensor(prob[:, :, 0:3:2, :], by_tile(XA).rearrange("p (h two) s -> p h two s", two=2),
                                        con[:, K_NEG:K_NEG + P].unsqueeze(1).unsqueeze(1).broadcast_to([P, HPG, 2, P]),
                                        ALU.add).then_inc(sig("scores_masked"), 1)
                dve.wait_ge(sig("scores_masked"), g + 1)
                nc.vector.tensor_reduce(stat[:, 16:16 + HPG], prob[:, :, 0, :], AX.X, ALU.max)
                dve.wait_ge(sig("scores_copied"), g + 1)
                nc.vector.tensor_reduce(stat[:, 16 + HPG:16 + 2 * HPG], prob[:, :, 1:3, :], AX.XY, ALU.max)\
                  .then_inc(sig("max_found"), 1)
                dve.wait_ge(sig("max_found"), g + 1)
                nc.vector.tensor_scalar(stat[:, 16:24], stat[:, 16:24], -SCALE, None, ALU.mult)\
                  .then_inc(sig("max_ready"), 1)
                dve.wait_ge(sig("ada_summed_a"), g + 1)
                piece(g * ADA_A, "a")
                steps(15, 21)
                dve.wait_ge(sig("exps"), g * 8 + 8)
                nc.vector.reciprocal(stat[:, 24:32], stat[:, 24:32]).then_inc(sig("sums_inverted"), 1)
                steps(21, 23)
                dve.wait_ge(sig("ada_summed_b"), g + 1)
                piece(g * ADA_A + 1, "b")
                dve.wait_ge(sig("att_summed"), g + 1)
                dve.wait_ge(sig("sums_inverted"), g + 1)
                nc.vector.tensor_tensor(side[:].rearrange("p t (h c) -> p (t h) c", c=P), by_tile(XB),
                                        stat[:, 24:32].unsqueeze(2).broadcast_to([P, 2 * HPG, P]), ALU.mult)\
                  .then_inc(sig("att_scaled"), 1)
                steps(23, 25)
                dve.wait_ge(sig("att_high"), g + 1)
                nc.vector.tensor_tensor(attT_lo[:], by_ktile(XA), attT_hi[:].bitcast(F32), ALU.subtract)\
                  .then_inc(sig("att_low"), 1)
                steps(25, 27)
                steps(27, 28)
                for i in range(2 * HPG):
                    dve.wait_ge(sig("log_f"), g * HPG + (i // TT + 1))
                    nc.vector.tensor_tensor_scan(bT[:, i], ones, bT[:, i], 0.0, ALU.mult, ALU.add)\
                      .then_inc(sig("b_ready"), 1)
                steps(28, 30)
                dve.wait_ge(sig("q_sigmoid"), g + 1)
                nc.vector.tensor_tensor(qT[:], qT[:], by_tile(XA), ALU.mult).then_inc(sig("q_ready"), 1)

                def decay(L):
                    view = tiles if L == len(LEVELS) else lambda f: halves(f, LEVELS[L])
                    d, z = view(dec[:, L % 2]), view(zT[:, L % 2])
                    n = len(LEVELS) + 2
                    dve.wait_ge(sig("decays"), g * n + (L + 1 + (L == len(LEVELS))))
                    if L == 0:
                        dve.wait_ge(sig("q_ready"), g + 1)
                        dve.wait_ge(sig("k_ready"), g * HPG + HPG)
                    if L >= 2:
                        dve.wait_ge(sig(f"level{L - 2}_scored"), g + 1)
                    nc.vector.tensor_tensor(z[:, :, 1, :], view(flat(qT))[:, :, 1, :], d[:, :, 1, :], ALU.mult)
                    nc.vector.tensor_tensor(z[:, :, 0, :], view(flat(kT))[:, :, 0, :], d[:, :, 0, :], ALU.mult)\
                      .then_inc(sig("decayed"), 1)

                def merge(L):
                    m = LEVELS[L]
                    dve.wait_ge(sig("masks_loaded"), 16)
                    dve.wait_ge(sig(f"level{L}_scored"), g + 1)
                    dve.wait_ge(sig(f"level{L - 1}_merged" if L else "self_merged"), g + 1)
                    shape = [P, 2 * HPG, P // (2 * m), m]
                    o = pT[:].rearrange("p i (x two m) -> p i x two m", two=2, m=m)[:, :, :, 1, :]
                    mask = msk[:, L * 64:(L + 1) * 64].rearrange("p (x m) -> p x m", m=m)
                    nc.vector.copy_predicated(o, mask.unsqueeze(1).broadcast_to(shape),
                                              PS[:, XA + L % 4, :].rearrange("p (i x m) -> p i x m", i=2 * HPG, m=m))\
                      .then_inc(sig(f"level{L}_merged"), 1)

                for c in range(30, A_N + AHEAD):
                    steps(c, c + 1)
                    if c == DECAY[0] + 1:
                        dve.wait_ge(sig("masks_loaded"), 16)
                        dve.wait_ge(sig("self_scored"), g + 1)
                        nc.vector.copy_predicated(pT[:], msk[:, len(LEVELS) * 64:].unsqueeze(1)
                                                  .broadcast_to([P, 2 * HPG, P]), by_tile(XB))\
                          .then_inc(sig("self_merged"), 1)
                    if c - 1 in DECAY[:-1]:
                        merge(DECAY.index(c - 1))
                    if c in DECAY:
                        decay(DECAY.index(c))
                    if c == A_OM + 3:
                        dve.wait_ge(sig("og_sigmoid"), g + 1)
                        p = pl.pair(7)
                        nc.vector.tensor_tensor(side[:], side[:], banks(2 * p), ALU.mult).then_inc(pair_free[p], 1)
                        dve.wait_ge(pair_free[p], pl.freed(7) + 1)
                        s3 = side[:].rearrange("p t (h c) -> p (t h) c", c=P)
                        nc.vector.tensor_tensor(s3, s3, con[:, K_GHG:K_GHG + P].unsqueeze(1)
                                                .broadcast_to([P, 2 * HPG, P]), ALU.mult).then_inc(sig("og_ready"), 1)
                    if c == A_OH - 3:
                        dve.wait_ge(sig("o_squared"), g + 1)
                        nc.vector.tensor_reduce(stat[:, 32:40], dec[:, 0].rearrange("p (i s) -> p i s", s=P), AX.X,
                                                ALU.add).then_inc(sig("o_square_sum"), 1)
                        dve.wait_ge(sig("o_square_sum"), g + 1)
                        rsqrt_of(stat[:, 32:40], P, "o", g)
                        nc.vector.tensor_tensor(dec[:, 1].rearrange("p (i s) -> p i s", s=P), by_tile(XB),
                                                stat[:, 32:40].unsqueeze(2).broadcast_to([P, 2 * HPG, P]), ALU.mult)\
                          .then_inc(sig("o_normed"), 1)
                        dve.wait_ge(sig("o_normed"), g + 1)
                        dve.wait_ge(sig("og_ready"), g + 1)
                        nc.vector.tensor_tensor(stage[:], gates(1), side[:], ALU.mult).then_inc(sig("o_gated"), 1)
                    if c == A_OH:
                        dve.wait_ge(sig("o_high"), g + 1)
                        nc.vector.tensor_tensor(oT_lo[:], by_ktile(XA), oT_hi[:].bitcast(F32), ALU.subtract)\
                          .then_inc(sig("o_low"), 1)
                    if c == A_OH + 3:
                        dve.wait_ge(sig("ada_summed_c"), g + 1)
                        piece(g * ADA_A + 2, "c")
                    n, odd = divmod(c - 3 - A_OM, CR)
                    if odd == CR - 1 and 0 <= n < 2 * GD:
                        dve.wait_ge(sig("sums_zeroed"), 2)
                        sums_of = yb if n < GD else ya
                        add_pair(pl, 8 + n, c - 3, sums_of[:, :, (n % GD) * NW:(n % GD + 1) * NW])

            def make_gain(which, c_gain, piece_at):
                nc.vector.tensor_tensor(gain_y[:], vec[:, c_gain:c_gain + KD], mods[:, piece_at:piece_at + KD],
                                        ALU.mult).then_inc(sig("gain_ready"), 1)
                dve.wait_ge(sig("gain_ready"), which)
                for k in range(KD):
                    nc.vector.tensor_scalar(diagonal(k), ident, gain_y[:, k:k + 1], None, ALU.mult)\
                      .then_inc(sig("gain_diagonal"), 1)

            dve.wait_ge(sig("mods_c"), NG)
            make_gain(1, C_GPOST, GA_M)
            with dve.Fori(0, GD) as n:
                pl = place_gate(n)
                cols = bass.ds(n * NW, NW)
                for c in range(AHEAD, 2 * CD + AHEAD):
                    low(pl, c)
                    i = c - G_ADA
                    if i == 0:
                        dve.wait_ge(sig("ada_summed_c"), NG)
                    if 0 <= i < CD:
                        ada_chunk(n + ADA_GATE, i, 0)
                    if c == CD + 3:
                        dve.wait_ge(pair_free[pl.pair(0)], pl.freed(0) + 1)
                        nc.vector.tensor_tensor(gates(0), gates(0), ya[:, :, cols], ALU.mult)\
                          .then_inc(sig("gated_a"), 1)
                dve.wait_ge(sig("ada_summed_d"), n + 1)
                piece(n + ADA_GATE, "d")
                dve.wait_ge(pair_free[pl.pair(1)], pl.freed(1) + 1)
                nc.vector.tensor_tensor(gates(1), gates(1), yb[:, :, cols], ALU.mult).then_inc(sig("gated_b"), 1)
                dve.wait_ge(sig("gated_a"), n + 1)
                dve.wait_ge(sig("gated_b"), n + 1)
                nc.vector.tensor_tensor(ya[:, :, cols], gates(0), gates(1), ALU.add).then_inc(sig("gated"), 1)

            for kp in range(KD // 2):
                dve.wait_ge(sig("m_high"), kp + 1)
                nc.vector.tensor_tensor(pairs(hT_lo, kp), PS[:, XA + kp % 4, :], pairs(hT_hi, kp).bitcast(F32),
                                        ALU.subtract).then_inc(sig("m_low"), 1)

            dve.wait_ge(sig("mods_d"), GD)
            nc.vector.scalar_tensor_tensor(out=scale_h[:], in0=mods[:, SC_F:SC_F + KD], scalar=1.0,
                                           in1=vec[:, C_GPRE2:C_GPRE2 + KD], op0=ALU.add, op1=ALU.mult)\
              .then_inc(sig("scale_h_ready"), 1)
            with dve.Fori(0, GD // 2) as n:
                pl = place_out(n)
                for j in range(2):
                    for c in range(j * CD + AHEAD, (j + 1) * CD + AHEAD):
                        low(pl, c)
                    dve.wait_ge(multiplied, pl.through((j + 1) * CD - 1))
                    p = pl.pair(j)
                    dve.wait_ge(sig("y_squared"), n * (2 * TT) + (j + 1) * TT)
                    nc.vector.tensor_tensor(ya[:, :, bass.ds(n * (2 * NW) + j * NW, NW)], banks(2 * p),
                                            gain_row[:, bass.ds(n * (2 * NW) + j * NW, NW)].unsqueeze(1)
                                            .broadcast_to([P, TT, NW]), ALU.mult)\
                      .then_inc(pair_free[p], 1)

            def reciprocal_rms(at, count, between=None):
                nc.vector.tensor_reduce(stat[:, at:at + TT], sums[:], AX.X, ALU.add)\
                  .then_inc(sig("squares_summed"), 1)
                dve.wait_ge(sig("squares_summed"), 1 if count == 1 else 2)
                rsqrt_of(stat[:, at:at + TT], D, "trunk", count, between)

            reciprocal_rms(8, 1)
            dve.wait_ge(sig("x_again"), 16)
            dve.wait_ge(pair_free[0], freed_by(0, G_FF))
            dve.wait_ge(pair_free[1], freed_by(1, G_FF))
            for tt in range(TT):
                nc.vector.scalar_tensor_tensor(out=yb[:, tt], in0=ya[:, tt], scalar=stat[:, 8 + tt:9 + tt],
                                               in1=yb[:, tt], op0=ALU.mult, op1=ALU.add)\
                  .then_inc(sig("x_mixed"), 1)
            dve.wait_ge(sig("x2_squared"), TT)
            rsqrt_of(stat[:, 10:10 + TT], D, "trunk", 2)
            for tt in range(TT):
                nc.vector.tensor_scalar(by_rms[:, tt], ident, stat[:, 10 + tt:11 + tt], None, ALU.mult)\
                  .then_inc(sig("rms_diagonal"), 1)
            dve.wait_ge(sig("scale_h_ready"), QUARTERS + 1)

            def h2_low(kp):
                dve.wait_ge(sig("h2_high"), kp + 1)
                nc.vector.tensor_tensor(pairs(hT_lo, kp), dec[:, kp % 2, 0:NW], pairs(hT_hi, kp).bitcast(F32),
                                        ALU.subtract).then_inc(sig("h2_low"), 1)

            first = Place(B_FF, G_FF)
            for kp in range(KD // 2):
                if kp == 0 or kp > AHEAD:
                    low(first, max(kp, AHEAD))
                dve.wait_ge(sig("x2_transposed"), kp + 1)
                if kp >= 2:
                    dve.wait_ge(sig("h2_low"), kp - 1)
                for j in range(2):
                    k = 2 * kp + j
                    nc.vector.tensor_scalar(dec[:, kp % 2, j * T:(j + 1) * T], PS[:, XA + kp % 4, j * T:(j + 1) * T],
                                            scale_h[:, k:k + 1], mods[:, SH_F + k:SH_F + k + 1], ALU.mult, ALU.add)\
                      .then_inc(sig("h2_scaled"), 1)
                if kp:
                    h2_low(kp - 1)
            h2_low(KD // 2 - 1)

            def hidden(pl):
                dve.wait_ge(multiplied, pl.through(-1))
                p = pl.pair(-1)
                nc.vector.tensor_tensor(stage[:], stage[:], banks(2 * p), ALU.mult).then_inc(pair_free[p], 1)

            def hidden_low(n):
                dve.wait_ge(sig("ff_high"), n)
                nc.vector.tensor_tensor(oT_lo[:], by_ktile(XA), oT_hi[:].bitcast(F32), ALU.subtract)\
                  .then_inc(sig("ff_low"), 1)

            def silu_gate(pl, n):
                dve.wait_ge(sig("ff_sigmoid"), n)
                p = pl.pair(0)
                nc.vector.tensor_tensor(stage[:], stage[:], banks(2 * p), ALU.mult).then_inc(pair_free[p], 1)

            for c in range(CD, 2 * CD):
                low(first, c)
                if c == CD + 3:
                    silu_gate(first, 1)
            make_gain(2, C_GPOST2, GA_F)
            with dve.Fori(1, NF) as n:
                pl = place_ff(n)
                for c in range(F_N):
                    low(pl, c)
                    if c == 3:
                        hidden(pl)
                    if c == 6:
                        hidden_low(n)
                    if c == CD + 3:
                        silu_gate(pl, n + 1)
                    j = c - CD - CR - 2
                    if j == 0:
                        dve.wait_ge(sig("sums_zeroed"), 3)
                    if j in (0, 2, 4, 6):
                        j //= 2
                        add_pair(pl, 1 + j, CD + j * CR + CR - 1, ya[:, :, j * NW:(j + 1) * NW])
            pl = Place(B_LAST, G_LAST)

            def add_out(j):
                dve.wait_ge(multiplied, pl.through(j * CR + CR - 1))
                cols = slice(j * NW, (j + 1) * NW)
                p = pl.pair(j)
                nc.vector.tensor_tensor(ya[:, :, cols], ya[:, :, cols], banks(2 * p), ALU.add)\
                  .then_inc(pair_free[p], 1)
                dve.wait_ge(pair_free[p], pl.freed(j) + 1)

            def gain_out(j):
                cols = slice(j * NW, (j + 1) * NW)
                dve.wait_ge(sig("y2_squared"), (j + 1) * TT)
                nc.vector.tensor_tensor(ya[:, :, cols], ya[:, :, cols], PS[:, XA + j, :].unsqueeze(1)
                                        .broadcast_to([P, TT, NW]), ALU.mult).then_inc(sig("y2_gained"), 1)

            for c in range(GD * CR):
                low(pl, c)
                if c == 3:
                    hidden(pl)
                    hidden_low(NF)
                if c in (4, 6):
                    add_out((c - 4) // 2)
            dve.wait_ge(sig("gain_spread"), 2)
            gain_out(0)
            for j in range(2, GD):
                add_out(j)
                gain_out(j - 1)
            dve.wait_ge(sig("y2_squared"), GD * TT)
            reciprocal_rms(12, 3, lambda: gain_out(GD - 1))
            for n in range(GD):
                cols = slice(n * NW, (n + 1) * NW)
                dve.wait_ge(sig("y2_gained"), n + 1)
                for tt in range(TT):
                    nc.vector.scalar_tensor_tensor(out=yb[:, tt, cols], in0=ya[:, tt, cols],
                                                   scalar=stat[:, 12 + tt:13 + tt], in1=yb[:, tt, cols],
                                                   op0=ALU.mult, op1=ALU.add).then_inc(sig("x_final"), 1)


def _by_columns(w, width=NW):
    k, n = w.shape
    return w.reshape(k // (KC * P), KC, P, n // width, width).transpose(3, 0, 2, 1, 4)\
            .reshape(n // width, k // (KC * P), P, KC * width)


def _by_rows(w):
    k, n = w.shape
    return w.reshape(k // NW, CR, KC, P, n // NW, NW).transpose(0, 4, 1, 3, 2, 5)\
            .reshape(k // NW, n // NW, CR, P, KC * NW)


def _columns(a):
    return a.reshape(-1, P).T


def kernel(x, c, positions, w_ada, b_ada, g_pre_mix, w_in, lb_logits, g_hg_out, w_o_hg, g_q_lora, w_uq,
           g_kv_lora, w_ukv, w_o_mla, w_out, g_post_mix, g_pre_ffn, w_gate_up, w_down, g_post_ffn):
    import concourse.bacc as bacc
    import numpy as np
    from concourse.bass_utils import run_bass_kernel_spmd

    f32 = np.float32
    (x, c, positions, w_ada, b_ada, g_pre_mix, w_in, lb_logits, g_hg_out, w_o_hg, g_q_lora, w_uq, g_kv_lora,
     w_ukv, w_o_mla, w_out, g_post_mix, g_pre_ffn, w_gate_up, w_down, g_post_ffn) = (
        np.asarray(a) for a in (x, c, positions, w_ada, b_ada, g_pre_mix, w_in, lb_logits, g_hg_out, w_o_hg,
                                g_q_lora, w_uq, g_kv_lora, w_ukv, w_o_mla, w_out, g_post_mix, g_pre_ffn,
                                w_gate_up, w_down, g_post_ffn))
    vectors = np.concatenate([_columns(a) for a in (c[0], b_ada[0], g_pre_mix[0], g_post_mix[0], g_pre_ffn[0],
                                                    g_post_ffn[0], g_q_lora[0], g_kv_lora[0], lb_logits[0],
                                                    lb_logits[1])], axis=1)
    i = np.arange(P)
    freq = (np.float32(10000.0) ** (-np.arange(0, ROPE, 2, dtype=f32) / f32(ROPE))).astype(f32)
    consts = np.concatenate([np.eye(P, dtype=f32), np.where(i[None, :] <= i[:, None], 0, -1e30).astype(f32),
                             np.ones((P, P), f32), np.broadcast_to(g_hg_out[0], (P, P)),
                             np.broadcast_to(freq, (P, HR)), np.full((P, TT * HPG), -0.5, f32)], axis=1)
    masks = np.zeros((P, len(LEVELS) * 64 + P), np.int32)
    for L, m in enumerate(LEVELS):
        j = np.arange(64)
        t = j // m * 2 * m + m + j % m
        masks[:, L * 64:(L + 1) * 64] = (i[:, None] // (2 * m) == t[None, :] // (2 * m)) & (i[:, None] % (2 * m) < m)
    masks[:, len(LEVELS) * 64:] = np.eye(P, dtype=np.int32)

    w_in, w_ada, w_uq, w_ukv, w_gate_up = w_in[0], w_ada[0], w_uq[0], w_ukv[0], w_gate_up[0]
    heads = D // P
    uq = w_uq.reshape(LORA, heads, P + ROPE)
    ukv = w_ukv.reshape(LORA, heads, 2 * P)
    ada = _by_columns(w_ada)
    at = 4 * D
    host = {
        "x": x[0].reshape(TT, P, D).transpose(1, 0, 2),
        "vectors": vectors, "consts": consts, "masks": masks, "positions": positions[0].reshape(TT, P).T,
        "ada0": ada[:2 * GD].reshape(2, GD, CD, P, KC * NW).transpose(1, 0, 2, 3, 4).reshape(-1, P, KC * NW), "ada1": ada[2 * GD:].reshape(-1, P, KC * NW),
        "w_c": _by_columns(w_in[:, at:at + 2 * LORA]).reshape(2, GD, CD // GD, P, KC * NW)
                           .transpose(1, 0, 2, 3, 4).reshape(-1, P, KC * NW),
        "w_kr": w_in[:, at + 2 * LORA:at + 2 * LORA + ROPE].reshape(KD, P, ROPE).transpose(1, 0, 2).reshape(P, KD * ROPE),
        "w_uqn": _by_columns(uq[:, :, :P].reshape(LORA, -1)),
        "w_uqr": _by_columns(uq[:, :, P:].reshape(LORA, -1), NW // 2),
        "w_uk": _by_columns(ukv[:, :, :P].reshape(LORA, -1)),
        "w_uv": _by_columns(ukv[:, :, P:].reshape(LORA, -1)),
        "w_hf": _by_columns(w_in[:, D:2 * D]), "w_hq": _by_columns(w_in[:, :D]),
        "w_hi": _by_columns(w_in[:, 2 * D:3 * D]), "w_hg": _by_columns(w_in[:, 3 * D:4 * D]),
        "w_omla": _by_rows(w_o_mla[0]), "w_ohg": _by_rows(w_o_hg[0]),
        "w_ga": _by_columns(w_in[:, -2 * D:-D]), "w_gb": _by_columns(w_in[:, -D:]),
        "w_out": _by_columns(w_out[0]),
        "w_gate": _by_columns(w_gate_up[:, :D_FF]), "w_up": _by_columns(w_gate_up[:, D_FF:]),
        "w_down": _by_rows(w_down[0]),
    }
    nc = bacc.Bacc("TRN2", target_bir_lowering=False, num_devices=1, dynamic_dma_scratch_size=1024)
    arrays, args = {}, []
    for name, a in host.items():
        a = np.ascontiguousarray(a)
        arrays["in_" + name] = a
        args.append(nc.dram_tensor("in_" + name, a.shape, mybir.dt.from_np(a.dtype), kind="ExternalInput").ap())
    args.append(nc.dram_tensor("out", (P, TT, D), F32, kind="ExternalOutput").ap())
    build(nc, *args)
    y = run_bass_kernel_spmd(nc, [arrays], core_ids=[0]).results[0]["out"]
    return y.reshape(P, TT, D).transpose(1, 0, 2).reshape(1, T, D)
```
